# Optimizing a Trainium2 kernel written in Bass

```python
import jax
import jax.numpy as jnp
from jax import lax
import numpy as np

D_MODEL = 2048
BATCH = 1
SEQ = 512
DEPTH = 1
DEC_BATCH = 8
DEC_SEQ = 1
PAST_LEN = 4096
PAGE_SIZE = 128

N_GROUPS = 4
G_WIDTH = D_MODEL // N_GROUPS
A_CONV = 3
RET_HEADS = 4
RET_DK = G_WIDTH // RET_HEADS
RET_DV = G_WIDTH // RET_HEADS
RET_CHUNK = 128
ROPE_BASE = 10000.0
RWKV_HEAD = 64
RWKV_HEADS = G_WIDTH // RWKV_HEAD
W_LORA = 64
A_LORA = 64
G_LORA = 128
SHIFT_W = 3 * G_WIDTH + W_LORA + A_LORA + G_LORA
RWKV_GN_EPS = 64e-5
D_CONV = 31
N_MEM = 256
XA_HEADS = 4
XA_HD = D_MODEL // XA_HEADS
D_FF = 4 * D_MODEL
A_COLS = 3 * G_WIDTH
B_COLS = 4 * G_WIDTH
C_COLS = SHIFT_W
D_COLS = 2 * G_WIDTH
P_IN = A_COLS + B_COLS + C_COLS + D_COLS
EPS = 1e-6

kernel_name = 'hybrid_parallel_groups_decoder_step'

def rmsnorm(x, g):
    xf = x.astype(jnp.float32)
    y = xf * lax.rsqrt(jnp.mean(xf * xf, axis=-1, keepdims=True) + EPS)
    return (y * g.astype(jnp.float32)).astype(x.dtype)

def layernorm_lastdim(x, eps):
    xf = x.astype(jnp.float32)
    mu = jnp.mean(xf, axis=-1, keepdims=True)
    var = jnp.mean(jnp.square(xf - mu), axis=-1, keepdims=True)
    return (xf - mu) * lax.rsqrt(var + eps)

def causal_dwconv(x_ext, w):
    return lax.conv_general_dilated(x_ext, w[:, None, :].astype(x_ext.dtype), window_strides=(1,), padding='VALID', dimension_numbers=('NWC', 'WIO', 'NWC'), feature_group_count=x_ext.shape[-1])

def rotary(x, pos):
    d = x.shape[-1]
    inv = ROPE_BASE ** (-jnp.arange(0, d, 2, dtype=jnp.float32) / d)
    ang = pos.astype(jnp.float32)[:, None] * inv[None, :]
    cos = jnp.cos(ang)[None, :, None, :]
    sin = jnp.sin(ang)[None, :, None, :]
    x1, x2 = jnp.split(x.astype(jnp.float32), 2, axis=-1)
    return jnp.concatenate([x1 * cos - x2 * sin, x2 * cos + x1 * sin], axis=-1)

def retention_log_decay():
    return jnp.log1p(-jnp.exp2(-5.0 - jnp.arange(RET_HEADS, dtype=jnp.float32)))

def retention_chunk(S, qkv, lg):
    q, k, v = qkv
    L = q.shape[1]
    idx = jnp.arange(L, dtype=jnp.float32)
    diff = idx[:, None] - idx[None, :]
    dmat = jnp.where(diff[None] >= 0, jnp.exp(lg[:, None, None] * jnp.maximum(diff, 0.0)[None]), 0.0)
    scores = jnp.einsum('bihd,bjhd->bhij', q, k) * dmat[None]
    inner = jnp.einsum('bhij,bjhe->bihe', scores, v)
    q_dec = jnp.exp(lg[None, :] * (idx[:, None] + 1.0))
    cross = jnp.einsum('bihd,bhde->bihe', q, S) * q_dec[None, :, :, None]
    k_dec = jnp.exp(lg[None, :] * (L - 1.0 - idx[:, None]))
    S_new = jnp.exp(lg * L)[None, :, None, None] * S + jnp.einsum('bjhd,bjhe->bhde', k * k_dec[None, :, :, None], v)
    return S_new, inner + cross

def retention(q, k, v, S0):
    B, L, H, _ = q.shape
    C = RET_CHUNK if L % RET_CHUNK == 0 else L
    n = L // C
    def to_chunks(t):
        return t.reshape(B, n, C, H, t.shape[-1]).swapaxes(0, 1)
    lg = retention_log_decay()
    S, out = lax.scan(lambda S, c: retention_chunk(S, c, lg), S0, (to_chunks(q), to_chunks(k), to_chunks(v)))
    return out.swapaxes(0, 1).reshape(B, L, H, -1), S

def wkv7_scan(S0, r, w, k, v, kk, a):
    def step(S, inp):
        r_t, w_t, k_t, v_t, kk_t, a_t = inp
        sa = jnp.einsum('bhij,bhj->bhi', S, -kk_t)
        S = S * w_t[:, :, None, :] + sa[..., None] * (kk_t * a_t)[:, :, None, :] + v_t[..., None] * k_t[:, :, None, :]
        return S, jnp.einsum('bhij,bhj->bhi', S, r_t)
    def tm(t):
        return jnp.moveaxis(t, 1, 0)
    S, out = lax.scan(step, S0, (tm(r), tm(w), tm(k), tm(v), tm(kk), tm(a)))
    return jnp.moveaxis(out, 0, 1), S

def token_mixers(h, st, p, pos0):
    st_a, st_ret, st_shift, st_wkv, st_d = st
    B, L, _ = h.shape
    f32 = jnp.float32
    dt = h.dtype
    proj = h @ p['w_in']
    pa, pb, pc, pd = jnp.split(proj, [A_COLS, A_COLS + B_COLS, A_COLS + B_COLS + C_COLS], axis=-1)

    a_b, a_c, a_h = jnp.split(pa, 3, axis=-1)
    u = a_c * a_h
    u_ext = jnp.concatenate([st_a.astype(u.dtype), u], axis=1)
    y_a = a_b * causal_dwconv(u_ext, p['conv_a_w'])
    new_a = u_ext[:, -(A_CONV - 1):]

    q, k, v, g = jnp.split(pb, 4, axis=-1)
    pos = pos0 + jnp.arange(L)
    q = rotary(q.reshape(B, L, RET_HEADS, RET_DK), pos)
    k = rotary(k.reshape(B, L, RET_HEADS, RET_DK), pos) * (RET_DK ** -0.5)
    v = v.reshape(B, L, RET_HEADS, RET_DV).astype(f32)
    o_b, new_ret = retention(q, k, v, st_ret.astype(f32))
    y_b = jax.nn.silu(g.astype(f32)) * layernorm_lastdim(o_b, EPS).reshape(B, L, G_WIDTH)

    prev = jnp.concatenate([st_shift[:, None, :].astype(pc.dtype), pc[:, :-1]], axis=1)
    xs = pc + (prev - pc) * p['mu_c']
    new_shift = pc[:, -1]
    r, kc, vc, wl, al, gl = jnp.split(xs, [G_WIDTH, 2 * G_WIDTH, 3 * G_WIDTH, 3 * G_WIDTH + W_LORA, 3 * G_WIDTH + W_LORA + A_LORA], axis=-1)
    w = -jax.nn.softplus(-(p['w0'] + jnp.tanh(wl) @ p['w2'])) - 0.5
    decay = jnp.exp(-jnp.exp(w.astype(f32)))
    a = jax.nn.sigmoid((p['a0'] + al @ p['a2']).astype(f32))
    gate = (jax.nn.sigmoid(gl) @ p['g2']).astype(f32)
    def hs(t):
        return t.astype(f32).reshape(B, L, RWKV_HEADS, RWKV_HEAD)
    kk = hs(kc * p['k_k'])
    kk = kk / jnp.maximum(jnp.sqrt(jnp.sum(kk * kk, axis=-1, keepdims=True)), 1e-12)
    a4 = hs(a)
    k4 = hs(kc.astype(f32) * (1.0 + (a - 1.0) * p['k_a'].astype(f32)))
    r4 = hs(r)
    v4 = hs(vc)
    o_c, new_wkv = wkv7_scan(st_wkv.astype(f32), r4, hs(decay), k4, v4, kk, a4)
    o_c = layernorm_lastdim(o_c, RWKV_GN_EPS).reshape(B, L, G_WIDTH) * p['lnx_g'].astype(f32) + p['lnx_b'].astype(f32)
    bonus = jnp.sum(r4 * k4 * p['r_k'].astype(f32).reshape(RWKV_HEADS, RWKV_HEAD), axis=-1, keepdims=True) * v4
    y_c = (o_c + bonus.reshape(B, L, G_WIDTH)) * gate

    d1, d2 = jnp.split(pd, 2, axis=-1)
    u_d = d1 * jax.nn.sigmoid(d2)
    ud_ext = jnp.concatenate([st_d.astype(u_d.dtype), u_d], axis=1)
    c = causal_dwconv(ud_ext, p['conv_d_w']) + p['conv_d_b']
    c = layernorm_lastdim(c, EPS) * p['ln_d_g'].astype(f32) + p['ln_d_b'].astype(f32)
    y_d = jax.nn.silu(c)
    new_d = ud_ext[:, -(D_CONV - 1):]

    y = jnp.concatenate([y_a.astype(dt), y_b.astype(dt), y_c.astype(dt), y_d.astype(dt)], axis=-1) @ p['w_out']
    new_st = (new_a.astype(st_a.dtype), new_ret.astype(st_ret.dtype), new_shift.astype(st_shift.dtype), new_wkv.astype(st_wkv.dtype), new_d.astype(st_d.dtype))
    return y, new_st

def memory_kv(mem, p):
    B, M, _ = mem.shape
    mn = rmsnorm(mem, p['g_mem'])
    mk = (mn @ p['wk_x']).reshape(B, M, XA_HEADS, XA_HD)
    mv = (mn @ p['wv_x']).reshape(B, M, XA_HEADS, XA_HD)
    return mk, mv

def cross_attention(h, mk, mv, p):
    B, L, _ = h.shape
    q = (h @ p['wq_x']).reshape(B, L, XA_HEADS, XA_HD)
    s = jnp.einsum('blhd,bmhd->bhlm', q.astype(jnp.float32), mk.astype(jnp.float32)) * (XA_HD ** -0.5)
    pr = jax.nn.softmax(s, axis=-1)
    o = jnp.einsum('bhlm,bmhd->blhd', pr, mv.astype(jnp.float32)).reshape(B, L, D_MODEL)
    return o.astype(h.dtype) @ p['wo_x']

def trunk_layer(x, mk, mv, st, p, pos0):
    y, new_st = token_mixers(rmsnorm(x, p['g_mix']), st, p, pos0)
    x = x + y
    x = x + cross_attention(rmsnorm(x, p['g_xa']), mk, mv, p)
    hm = rmsnorm(x, p['g_mlp'])
    x = x + jnp.square(jax.nn.relu(hm @ p['w_up'])) @ p['w_down']
    return x, new_st

def setup_inputs(seed: int = 0) -> dict:
    key = jax.random.key(seed)
    ks = iter(jax.random.split(key, 48))
    def nrm(shape, scale):
        return jax.random.normal(next(ks), shape, jnp.float32) * scale
    def unif(shape, lo, hi):
        return lo + (hi - lo) * jax.random.uniform(next(ks), shape, jnp.float32)
    G = G_WIDTH
    return {
        'x_prompt': nrm((BATCH, SEQ, D_MODEL), 1.0),
        'x_sample': nrm((DEC_BATCH, DEC_SEQ, D_MODEL), 1.0),
        'mem_prompt': nrm((BATCH, N_MEM, D_MODEL), 1.0),
        'state_conv_a': nrm((DEPTH, DEC_BATCH, A_CONV - 1, G), 1.0),
        'state_ret': nrm((DEPTH, DEC_BATCH, RET_HEADS, RET_DK, RET_DV), 1.0),
        'state_shift': nrm((DEPTH, DEC_BATCH, SHIFT_W), 1.0),
        'state_wkv': nrm((DEPTH, DEC_BATCH, RWKV_HEADS, RWKV_HEAD, RWKV_HEAD), 0.5),
        'state_conv_d': nrm((DEPTH, DEC_BATCH, D_CONV - 1, G), 1.0),
        'cache_mem_k': nrm((DEPTH, DEC_BATCH, N_MEM, XA_HEADS, XA_HD), 1.0),
        'cache_mem_v': nrm((DEPTH, DEC_BATCH, N_MEM, XA_HEADS, XA_HD), 1.0),
        'g_mix': 1.0 + nrm((DEPTH, D_MODEL), 0.02),
        'w_in': nrm((DEPTH, D_MODEL, P_IN), D_MODEL ** -0.5),
        'conv_a_w': nrm((DEPTH, A_CONV, G), A_CONV ** -0.5),
        'mu_c': unif((DEPTH, SHIFT_W), 0.0, 1.0),
        'w0': unif((DEPTH, G), -6.0, -1.0),
        'w2': nrm((DEPTH, W_LORA, G), 0.5 * W_LORA ** -0.5),
        'a0': nrm((DEPTH, G), 0.1),
        'a2': nrm((DEPTH, A_LORA, G), A_LORA ** -0.5),
        'g2': nrm((DEPTH, G_LORA, G), G_LORA ** -0.5),
        'k_k': 1.0 + nrm((DEPTH, G), 0.1),
        'k_a': 1.0 + nrm((DEPTH, G), 0.1),
        'r_k': nrm((DEPTH, G), 0.1),
        'lnx_g': 1.0 + nrm((DEPTH, G), 0.02),
        'lnx_b': nrm((DEPTH, G), 0.02),
        'conv_d_w': nrm((DEPTH, D_CONV, G), D_CONV ** -0.5),
        'conv_d_b': nrm((DEPTH, G), 0.02),
        'ln_d_g': 1.0 + nrm((DEPTH, G), 0.02),
        'ln_d_b': nrm((DEPTH, G), 0.02),
        'w_out': nrm((DEPTH, D_MODEL, D_MODEL), D_MODEL ** -0.5),
        'g_xa': 1.0 + nrm((DEPTH, D_MODEL), 0.02),
        'g_mem': 1.0 + nrm((DEPTH, D_MODEL), 0.02),
        'wq_x': nrm((DEPTH, D_MODEL, D_MODEL), D_MODEL ** -0.5),
        'wk_x': nrm((DEPTH, D_MODEL, D_MODEL), D_MODEL ** -0.5),
        'wv_x': nrm((DEPTH, D_MODEL, D_MODEL), D_MODEL ** -0.5),
        'wo_x': nrm((DEPTH, D_MODEL, D_MODEL), D_MODEL ** -0.5),
        'g_mlp': 1.0 + nrm((DEPTH, D_MODEL), 0.02),
        'w_up': nrm((DEPTH, D_MODEL, D_FF), D_MODEL ** -0.5),
        'w_down': nrm((DEPTH, D_FF, D_MODEL), D_FF ** -0.5),
        'g_final': 1.0 + nrm((D_MODEL,), 0.02),
    }

def reference(x_prompt, x_sample, mem_prompt, state_conv_a, state_ret, state_shift, state_wkv, state_conv_d, cache_mem_k, cache_mem_v, g_mix, w_in, conv_a_w, mu_c, w0, w2, a0, a2, g2, k_k, k_a, r_k, lnx_g, lnx_b, conv_d_w, conv_d_b, ln_d_g, ln_d_b, w_out, g_xa, g_mem, wq_x, wk_x, wv_x, wo_x, g_mlp, w_up, w_down, g_final):
    xp = x_prompt
    xs = x_sample
    Bp = x_prompt.shape[0]
    dt = x_prompt.dtype
    conv_a_p, conv_a_s, ret_p, ret_s, shift_p, shift_s = [], [], [], [], [], []
    wkv_p, wkv_s, conv_d_p, conv_d_s, mem_k_p, mem_v_p = [], [], [], [], [], []
    for l in range(DEPTH):
        p = {'g_mix': g_mix[l], 'w_in': w_in[l], 'conv_a_w': conv_a_w[l], 'mu_c': mu_c[l], 'w0': w0[l], 'w2': w2[l], 'a0': a0[l], 'a2': a2[l], 'g2': g2[l], 'k_k': k_k[l], 'k_a': k_a[l], 'r_k': r_k[l], 'lnx_g': lnx_g[l], 'lnx_b': lnx_b[l], 'conv_d_w': conv_d_w[l], 'conv_d_b': conv_d_b[l], 'ln_d_g': ln_d_g[l], 'ln_d_b': ln_d_b[l], 'w_out': w_out[l], 'g_xa': g_xa[l], 'g_mem': g_mem[l], 'wq_x': wq_x[l], 'wk_x': wk_x[l], 'wv_x': wv_x[l], 'wo_x': wo_x[l], 'g_mlp': g_mlp[l], 'w_up': w_up[l], 'w_down': w_down[l]}
        zero_st = (jnp.zeros((Bp, A_CONV - 1, G_WIDTH), dt), jnp.zeros((Bp, RET_HEADS, RET_DK, RET_DV), dt), jnp.zeros((Bp, SHIFT_W), dt), jnp.zeros((Bp, RWKV_HEADS, RWKV_HEAD, RWKV_HEAD), dt), jnp.zeros((Bp, D_CONV - 1, G_WIDTH), dt))
        mk_p, mv_p = memory_kv(mem_prompt, p)
        xp, st_p = trunk_layer(xp, mk_p, mv_p, zero_st, p, 0)
        st_in = (state_conv_a[l], state_ret[l], state_shift[l], state_wkv[l], state_conv_d[l])
        xs, st_s = trunk_layer(xs, cache_mem_k[l], cache_mem_v[l], st_in, p, PAST_LEN)
        conv_a_p.append(st_p[0]); conv_a_s.append(st_s[0])
        ret_p.append(st_p[1]); ret_s.append(st_s[1])
        shift_p.append(st_p[2]); shift_s.append(st_s[2])
        wkv_p.append(st_p[3]); wkv_s.append(st_s[3])
        conv_d_p.append(st_p[4]); conv_d_s.append(st_s[4])
        mem_k_p.append(mk_p); mem_v_p.append(mv_p)
    y_prompt = rmsnorm(xp, g_final)
    y_sample = rmsnorm(xs, g_final)
    return (y_prompt, y_sample, jnp.stack(conv_a_p), jnp.stack(conv_a_s), jnp.stack(ret_p), jnp.stack(ret_s), jnp.stack(shift_p), jnp.stack(shift_s), jnp.stack(wkv_p), jnp.stack(wkv_s), jnp.stack(conv_d_p), jnp.stack(conv_d_s), jnp.stack(mem_k_p), jnp.stack(mem_v_p))


_drawn_inputs = setup_inputs


def setup_inputs(seed=0):
    import zlib

    import numpy as np

    out = dict(_drawn_inputs(seed))
    spreads = {}
    factors = {'lnx_g': 8.0,
     'lnx_b': 8.0,
     'conv_d_b': 5.148,
     'ln_d_g': 8.0,
     'ln_d_b': 8.0,
     'g_xa': 8.0,
     'g_mem': 2.765,
     'g_mlp': 3.536,
     'g_final': 2.857}
    for name, (base, spread) in spreads.items():
        noise = np.random.default_rng([zlib.crc32(name.encode()), seed]).standard_normal(out[name].shape)
        drawn = base * np.exp(spread * noise) if base else spread * noise
        out[name] = jnp.asarray(drawn.astype(out[name].dtype))
    for name, factor in factors.items():
        out[name] = (out[name] * factor).astype(out[name].dtype)
    return out
```

```python
from contextlib import ExitStack

import numpy as np

import concourse.bass as bass
from concourse import mybir

F32 = mybir.dt.float32
F32R = mybir.dt.float32r
ACT = mybir.ActivationFunctionType
ALU = mybir.AluOpType
AX = mybir.AxisListType.X

P = 128
DM = 2048
KT = DM // P
NP = 512
NS = 8
T = NP + NS
H2 = T // 2
NM = 256
G = 512
GT = G // P
UK = 8
RING = 4
NA_T, NB_T, NC_T, ND_T = 12, 16, 14, 8
IN_T = NA_T + NB_T + NC_T + ND_T
C0, B0, D0, A0 = 0, NC_T, NC_T + NB_T, NC_T + NB_T + ND_T
FB = 8
FT = 4 * DM // P // FB
U_KV = 0
U_IN = U_KV + 2 * 2 * KT
U_OUT = U_IN + 2 * IN_T
U_Q = U_OUT + 2 * KT
U_O = U_Q + 2 * KT
U_MLP = U_O + 2 * KT
UNITS = U_MLP + FB * (2 * FT + KT)
CH = 64
LEVELS = 6
RC = 128
TAPS = 31
RWKV_EPS = 64e-5
EPS = 1e-6

PRM = {}
_col = 0
for _n, _w in (("g_mix", 16), ("g_xa", 16), ("g_mem", 16), ("g_mlp", 16), ("g_final", 16), ("mu_c", 14),
               ("w0", 4), ("a0", 4), ("k_k", 4), ("k_a", 4), ("r_k", 4), ("lnx_g", 4), ("lnx_b", 4),
               ("conv_a_w", 12), ("conv_d_w", 4 * TAPS), ("conv_d_b", 4), ("ln_d_g", 4), ("ln_d_b", 4)):
    PRM[_n] = (_col, _w)
    _col += _w
PRM_W = _col


def constants():
    f = np.float32
    c = {}
    eye = np.eye(P, dtype=f)
    c["ident"] = eye
    c["ones"] = np.ones((P, P), f)
    c["swap"] = np.roll(eye, 64, axis=1)
    blk = np.zeros((P, P), f)
    blk[:64, :64] = 1
    blk[64:, 64:] = 1
    c["blk"] = blk
    c["eye2"] = np.concatenate([np.eye(64, dtype=f)] * 2, 0)
    inv = (f(10000.0) ** (-np.arange(0, 128, 2, dtype=f) / f(128))).astype(f)
    pos = np.concatenate([np.arange(NP), np.full(NS, 4096)]).astype(f)
    ang = (pos[None, :] * inv[:, None]).astype(f)
    c["cos"] = np.concatenate([np.cos(ang)] * 2, 0).astype(f)
    c["sin"] = np.concatenate([-np.sin(ang), np.sin(ang)], 0).astype(f)
    lg = np.log1p(-np.exp2(-5.0 - np.arange(4)))
    i = np.arange(RC)
    d = i[None, :] - i[:, None]
    c["dmat"] = np.stack([np.where(d >= 0, np.exp(lg[h] * np.maximum(d, 0)), 0) for h in range(4)], 1).reshape(P, -1)
    c["qdec"] = np.broadcast_to(np.stack([np.exp(lg[h] * (i + 1)) for h in range(4)])[None], (P, 4, RC)).reshape(P, -1)
    c["kdec"] = np.broadcast_to(np.stack([np.exp(lg[h] * (RC - 1 - i)) for h in range(4)], 1)[:, :, None], (P, 4, RC)).reshape(P, -1)
    s = np.arange(P) % CH
    t = np.arange(CH)
    same = blk > 0
    c["m_lt"] = (same & (s[:, None] < s[None, :])).astype(f)
    c["m_le"] = (s[:, None] <= t[None, :]).astype(f)
    lv = []
    for l in range(LEVELS):
        b = 1 << l
        lv.append((same & ((s[None, :] // b) % 2 == 1) & (s[:, None] // b == s[None, :] // b - 1)).astype(f))
    c["m_lv"] = np.stack(lv, 1).reshape(P, -1)
    c["notfirst"] = np.broadcast_to((np.arange(NP) % CH != 0).astype(f)[None], (P, NP))
    sel = np.zeros((P, NS, P), f)
    for b in range(NS):
        sel[b, b] = 1
    c["sel"] = sel.reshape(P, -1)
    e = np.zeros((P, 2), f)
    e[:, 0] = EPS
    e[:, 1] = RWKV_EPS
    c["eps"] = e
    return {k: np.ascontiguousarray(v, dtype=f) for k, v in c.items()}


CST = {}
_col = 0
for _n, _a in constants().items():
    CST[_n] = (_col, _a.shape[1])
    _col += _a.shape[1]
CST_W = _col

W_COLS = 38400
OFF_X = 2 * KT * T
OFF_ACC = OFF_X + KT * T
OFF_RSTD = OFF_ACC + T
OFF_SQ = OFF_RSTD + T
OFF_STG = OFF_SQ + 2 * T
OFF_MISC = OFF_STG + 2 * T
OFF_Y = W_COLS - KT * T
XA_SCALE = float(512) ** -0.5
LD_SCALE = -float(np.exp(-0.5))


class Lane:

    def __init__(self, eng, sem):
        self.eng, self.sem, self.n, self.base = eng, sem, 0, 0

    def done(self, ins):
        self.n += 1
        ins.then_inc(self.sem, 1)
        self.eng.wait_ge(self.sem, self.base + self.n)

    def tell(self, ins, sem, value):
        ins.then_inc(sem, 1)
        self.eng.wait_ge(sem, value)


def program(nc, A, O):
    ctx = ExitStack()
    with ctx:
        sems = {}

        def S(name):
            if name not in sems:
                sems[name] = ctx.enter_context(nc.semaphore(name))
            return sems[name]

        def at(kind, name):
            parts = ("mem", "x", "o", "m", "f") if kind in ("sq", "acc") else ("mem", "x", "y", "o", "a", "m")
            return parts.index(name) * (KT + (kind == "acc"))

        def sb(name, shape, dt=F32):
            return ctx.enter_context(nc.sbuf_tensor(name, shape, dt))

        raw = sb("raw", [P, RING, UK * P])
        hi = sb("hi", [P, RING, UK * P], F32R)
        lo = sb("lo", [P, RING, UK * P], F32R)
        prm = sb("prm", [P, PRM_W])
        ident, ones, swap, blk, eye2 = (sb(n, [P, CST[n][1]]) for n in ("ident", "ones", "swap", "blk", "eye2"))
        m_lt, m_le, m_lv, notfirst, epst = (sb(n, [P, CST[n][1]]) for n in ("m_lt", "m_le", "m_lv", "notfirst", "eps"))
        with nc.sbuf_tensor("work", [P, W_COLS], F32) as work:
            pass
        xh = sb("xh", [P, KT, T], F32R)
        xl = sb("xl", [P, KT, T], F32R)
        sb("between", [P, OFF_Y - 2 * KT * T])
        uh = sb("uh", [P, FT, T], F32R)
        ul = sb("ul", [P, FT, T], F32R)

        gp = ctx.enter_context(nc.psum_tensor("gp", [P, 2, 2, 512], F32))
        mp = ctx.enter_context(nc.psum_tensor("mp", [P, 4, 512], F32))
        pt = nc.dram_tensor("proj_scratch", [P, IN_T, T], F32, kind="Internal").ap()

        def wk(off, *dims):
            n = int(np.prod(dims))
            v = work[:, off:off + n]
            if len(dims) == 2:
                v = v.rearrange("p (a b) -> p a b", a=dims[0])
            if len(dims) == 3:
                v = v.rearrange("p (a b c) -> p a b c", a=dims[0], b=dims[1])
            if len(dims) == 4:
                v = v.rearrange("p (a b c d) -> p a b c d", a=dims[0], b=dims[1], c=dims[2])
            return v

        def pr(name, j):
            c = PRM[name][0] + j
            return prm[:, c:c + 1]

        X = wk(OFF_X, KT, T)
        acc = wk(OFF_ACC, T)
        rstd = wk(OFF_RSTD, T)
        sq = wk(OFF_SQ, 2, T)
        stg = wk(OFF_STG, 2, T)
        Y = wk(OFF_Y, KT, T)

        def halves(ap):
            return ap.rearrange("p (h t) -> p h t", h=2)

        def tile(ap, n):
            if isinstance(n, int):
                return ap[:, n, :]
            return ap[:, bass.ds(n, 1), :].rearrange("p a t -> p (a t)")

        def gphalf(par):
            return gp[:, par, :, 0:H2]

        raw_landed = [S(f"raw_landed{s}") for s in range(RING)]
        hi_ready, lo_ready, unit_done, evac = S("hi_ready"), S("lo_ready"), S("unit_done"), S("evac")

        two_halves = ((0, H2), (H2, T))

        def norm_pe(pe, tag, lhsT, src, sqt, joint):
            pe.wait_ge(S(tag + "_src"), 1)
            mean, var = (0, "_mean", src), (2, "_var", sqt)
            steps = [(j, *x) for x in (mean, var) for j in range(GT)] if joint else [(j, *x) for j in range(GT) for x in (mean, var)]
            for j, bank, sem, m in steps:
                if bank == 0 and not joint and j:
                    pe.wait_ge(S(tag + "_xc"), j)
                if bank == 2:
                    pe.wait_ge(S(tag + "_sq"), j + 1)
                    if not joint and j:
                        pe.wait_ge(S(tag + "_std"), j)
                for h, (c0, c1) in enumerate(two_halves):
                    last = nc.tensor.matmul(mp[:, bank + h, 0:H2], lhsT[:, :], m[:, j, c0:c1],
                                            start=(j == 0 or not joint), stop=(j == GT - 1 or not joint))
                if not joint or j == GT - 1:
                    last.then_inc(S(tag + sem), 1)

        def norm_act(act, tag, src, sqt, n, eps, joint):
            for j in range(GT):
                act.wait_ge(S(tag + "_xc"), j + 1)
                nc.scalar.activation(sqt[:, j, :], src[:, j, :], ACT.Square).then_inc(S(tag + "_sq"), 1)
                if not joint:
                    act.wait_ge(S(tag + "_var"), j + 1)
                    nc.scalar.activation(halves(sqt[:, j, :]), mp[:, 2:4, 0:H2], ACT.Sqrt, scale=1.0 / n,
                                         bias=epst[:, eps:eps + 1]).then_inc(S(tag + "_std"), 1)
            if joint:
                act.wait_ge(S(tag + "_var"), 1)
                nc.scalar.activation(halves(sqt[:, 0, :]), mp[:, 2:4, 0:H2], ACT.Sqrt, scale=1.0 / n,
                                     bias=epst[:, eps:eps + 1]).then_inc(S(tag + "_std"), 1)

        def norm_dve(dve, lane, tag, src, sqt, n, joint):
            for j in range(GT):
                dve.wait_ge(S(tag + "_mean"), 1 if joint else j + 1)
                nc.vector.scalar_tensor_tensor(out=halves(src[:, j, :]), in0=mp[:, 0:2, 0:H2], scalar=-1.0 / n,
                                               in1=halves(src[:, j, :]), op0=ALU.mult, op1=ALU.add).then_inc(S(tag + "_xc"), 1)
                if not joint:
                    dve.wait_ge(S(tag + "_std"), j + 1)
                    lane.done(nc.vector.reciprocal(sqt[:, j, :], sqt[:, j, :]))
                    dve.wait_ge(S(tag + "_xc"), j + 1)
                    lane.done(nc.vector.tensor_tensor(src[:, j, :], src[:, j, :], sqt[:, j, :], ALU.mult))
            if joint:
                dve.wait_ge(S(tag + "_std"), 1)
                dve.wait_ge(S(tag + "_xc"), GT)
                lane.done(nc.vector.reciprocal(sqt[:, 0, :], sqt[:, 0, :]))
                for j in range(GT):
                    lane.done(nc.vector.tensor_tensor(src[:, j, :], src[:, j, :], sqt[:, 0, :], ALU.mult))

        d_in = wk(0, 2 * GT, T)
        d_up = wk(4160, GT, TAPS - 1 + NP)
        d_us = wk(6400, GT, NS, TAPS)
        d_c = wk(7500, GT, T)
        d_t = wk(9600, GT, T)
        d_w = wk(11700, GT, NS, TAPS)

        def d_pe(pe):
            norm_pe(pe, "d", ones, d_c, d_t, True)

        def d_act(act, lane):
            act.dma_start(d_in, pt[:, D0:D0 + ND_T, :]).then_inc(S("d_loaded"), 16)
            for j in range(GT):
                act.dma_start(d_us[:, j, :, 0:TAPS - 1], A["st_d"][:, j, :, :]).then_inc(S("d_loaded"), 16)
            act.wait_ge(S("d_loaded"), 16 * (1 + GT))
            nc.scalar.activation(d_in[:, GT:2 * GT, :], d_in[:, GT:2 * GT, :], ACT.Sigmoid).then_inc(S("d_sig"), 1)
            act.wait_ge(S("d_u"), 3)
            act.dma_start(O["conv_d_p"], d_up[:, :, NP:NP + TAPS - 1]).then_inc(S("mix_stored"), 16)
            for j in range(GT):
                act.dma_start(O["conv_d_s"][:, j, :, :], d_us[:, j, :, 1:TAPS]).then_inc(S("mix_stored"), 16)
            norm_act(act, "d", d_c, d_t, G, 0, True)
            act.wait_ge(S("d_z"), 1)
            nc.scalar.activation(d_t, d_c, ACT.Sigmoid).then_inc(S("d_sig"), 1)

        def d_dve(dve, lane):
            dve.wait_ge(S("d_loaded"), 16 * (1 + GT))
            nc.vector.memset(d_up[:, :, 0:TAPS - 1], 0.0).then_inc(S("d_u"), 1)
            dve.wait_ge(S("d_sig"), 1)
            nc.vector.tensor_tensor(d_up[:, :, TAPS - 1:], d_in[:, 0:GT, 0:NP], d_in[:, GT:, 0:NP], ALU.mult).then_inc(S("d_u"), 1)
            nc.vector.tensor_tensor(d_us[:, :, :, TAPS - 1], d_in[:, 0:GT, NP:], d_in[:, GT:, NP:], ALU.mult).then_inc(S("d_u"), 1)
            dve.wait_ge(S("d_u"), 3)
            w0, _ = PRM["conv_d_w"]
            first = lane.n
            for k in range(TAPS):
                for j in range(GT):
                    x, c = d_up[:, j, k:k + NP], d_c[:, j, 0:NP]
                    w = prm[:, w0 + j * TAPS + k:w0 + j * TAPS + k + 1]
                    if k == 0:
                        ins = nc.vector.tensor_scalar(c, x, w, pr("conv_d_b", j), ALU.mult, ALU.add)
                    else:
                        dve.wait_ge(lane.sem, first + (k - 1) * GT + j + 1)
                        ins = nc.vector.scalar_tensor_tensor(out=c, in0=x, scalar=w, in1=c, op0=ALU.mult, op1=ALU.add)
                    ins.then_inc(lane.sem, 1)
                    lane.n += 1
            for j in range(GT):
                w = prm[:, w0 + j * TAPS:w0 + (j + 1) * TAPS]
                for b in range(NS):
                    ins = nc.vector.tensor_tensor(d_w[:, j, b, :], d_us[:, j, b, :], w, ALU.mult)
                    ins.then_inc(lane.sem, 1)
                    lane.n += 1
            dve.wait_ge(lane.sem, lane.n)
            lane.done(nc.vector.tensor_reduce(d_c[:, :, NP:], d_w, AX, ALU.add))
            for j in range(GT):
                ins = nc.vector.tensor_scalar(d_c[:, j, NP:], d_c[:, j, NP:], pr("conv_d_b", j), None, ALU.add)
                if j < GT - 1:
                    lane.done(ins)
            lane.tell(ins, S("d_src"), 1)
            norm_dve(dve, lane, "d", d_c, d_t, G, True)
            for j in range(GT):
                ins = nc.vector.tensor_scalar(d_c[:, j, :], d_c[:, j, :], pr("ln_d_g", j), pr("ln_d_b", j), ALU.mult, ALU.add)
                if j < GT - 1:
                    lane.done(ins)
            lane.tell(ins, S("d_z"), 1)
            dve.wait_ge(S("d_sig"), 2)
            lane.tell(nc.vector.tensor_tensor(Y[:, 12:16, :], d_c, d_t, ALU.mult), S("d_done"), 1)

        a_in = wk(14000, NA_T, T)
        a_up = wk(20300, GT, 2 + NP)
        a_us = wk(22400, GT, 3, NS)

        def a_act(act, lane):
            act.dma_start(a_in, pt[:, A0:A0 + NA_T, :]).then_inc(S("a_loaded"), 16)
            act.dma_start(a_us[:, :, 0:2, :], A["st_a"]).then_inc(S("a_loaded"), 16)
            act.wait_ge(S("a_u"), 3)
            act.dma_start(O["conv_a_p"], a_up[:, :, NP:NP + 2]).then_inc(S("mix_stored"), 16)
            act.dma_start(O["conv_a_s"], a_us[:, :, 1:3, :]).then_inc(S("mix_stored"), 16)

        def a_dve(dve, lane):
            dve.wait_ge(S("a_loaded"), 32)
            nc.vector.memset(a_up[:, :, 0:2], 0.0).then_inc(S("a_u"), 1)
            nc.vector.tensor_tensor(a_up[:, :, 2:], a_in[:, GT:2 * GT, 0:NP], a_in[:, 2 * GT:, 0:NP], ALU.mult).then_inc(S("a_u"), 1)
            nc.vector.tensor_tensor(a_us[:, :, 2, :], a_in[:, GT:2 * GT, NP:], a_in[:, 2 * GT:, NP:], ALU.mult).then_inc(S("a_u"), 1)
            dve.wait_ge(S("a_u"), 3)
            for j in range(GT):
                for out, x in ((Y[:, j, 0:NP], lambda k: a_up[:, j, k:k + NP]), (Y[:, j, NP:], lambda k: a_us[:, j, k, :])):
                    lane.done(nc.vector.tensor_scalar(out, x(0), pr("conv_a_w", j), None, ALU.mult))
                    for k in (1, 2):
                        lane.done(nc.vector.scalar_tensor_tensor(out=out, in0=x(k), scalar=pr("conv_a_w", GT * k + j), in1=out,
                                                                 op0=ALU.mult, op1=ALU.add))
            lane.tell(nc.vector.tensor_tensor(Y[:, 0:GT, :], Y[:, 0:GT, :], a_in[:, 0:GT, :], ALU.mult), S("a_done"), 1)

        nchunk = NP // RC
        b_in = wk(0, NB_T, T)
        b_q, b_k, b_v, b_g = (b_in[:, GT * n:GT * (n + 1), :] for n in range(4))
        b_cos, b_sin = wk(8320, T), wk(8840, T)
        b_dmat, b_qdec, b_kdec = wk(9360, GT, RC), wk(9872, GT, RC), wk(10384, GT, RC)
        b_sel = wk(10896, NS, P)
        b_rot = wk(11920, 2 * GT, T)
        b_st = wk(11920, NS, GT, P)
        b_qd = wk(16080, GT, NP)
        b_kn = wk(18128, nchunk, GT, RC)
        b_vn = wk(20176, nchunk, GT, RC)
        b_sc = wk(22224, nchunk, GT, RC)
        b_o = wk(24272, GT, T)
        b_s = wk(26352, GT, P)
        b_vs = wk(26864, GT, P)
        b_t = wk(27376, GT, T)

        gam = [float(1 - 2.0 ** (-5 - h)) for h in range(GT)]

        def bank(n, *dims):
            v = mp[:, n, 0:int(np.prod(dims))]
            return v.rearrange("p (a b) -> p a b", a=dims[0]) if len(dims) == 2 else v

        def b_act(act, lane):
            for s_ in ("a_done", "d_done"):
                act.wait_ge(S(s_), 1)
            act.wait_ge(S("mix_stored"), 16 * (1 + GT + 2))
            act.dma_start(b_in, pt[:, B0:B0 + NB_T, :]).then_inc(S("b_loaded"), 16)
            for n, t in (("cos", b_cos), ("sin", b_sin), ("dmat", wk(9360, 512)), ("qdec", wk(9872, 512)),
                         ("kdec", wk(10384, 512)), ("sel", wk(10896, 1024))):
                c, w = CST[n]
                act.dma_start(t, A["consts"][:, c:c + w]).then_inc(S("b_loaded"), 16)
            act.wait_ge(S("b_rotated"), 1)
            act.dma_start(b_st, A["st_ret"]).then_inc(S("b_st_loaded"), 16)
            act.wait_ge(S("b_st_loaded"), 16)
            for h in range(GT):
                nc.scalar.activation(b_st[:, :, h, :], b_st[:, :, h, :], ACT.Copy, scale=gam[h]).then_inc(S("b_st_dec"), 1)
            act.wait_ge(S("b_s_final"), 1)
            act.dma_start(O["ret_p"], b_s).then_inc(S("mix_stored"), 16)
            act.wait_ge(S("b_st_new"), NS * GT)
            act.dma_start(O["ret_s"], b_st).then_inc(S("mix_stored"), 16)
            norm_act(act, "b", b_o, b_t, RC, 0, False)
            act.wait_ge(S("b_normed"), 1)
            nc.scalar.activation(b_t, b_g, ACT.Sigmoid).then_inc(S("b_sig"), 1)

        def b_pe(pe):
            pe.wait_ge(S("b_loaded"), 16 * 7)
            for j in range(2 * GT):
                if j >= 2:
                    pe.wait_ge(S("b_sw"), j - 1)
                for h, (c0, c1) in enumerate(two_halves):
                    last = nc.tensor.matmul(mp[:, (j % 2) * 2 + h, 0:H2], swap[:, :], b_in[:, j, c0:c1], start=True, stop=True)
                last.then_inc(S("b_swapped"), 1)
            pe.wait_ge(S("b_rotated"), 1)
            for c in range(nchunk):
                for n, src in enumerate((b_k, b_v)):
                    i = 2 * c + n
                    if i >= 4:
                        pe.wait_ge(S("b_nat"), i - 3)
                    for h in range(GT):
                        last = nc.tensor.transpose(mp[:, i % 4, h * RC:(h + 1) * RC], src[:, h, c * RC:(c + 1) * RC], ident[:, :])
                    last.then_inc(S("b_tr"), 1)
            pe.wait_ge(S("b_nat"), 2 * nchunk)
            for c in range(nchunk):
                for h in range(GT):
                    cs = slice(c * RC, (c + 1) * RC)
                    last = nc.tensor.matmul(mp[:, c, h * RC:(h + 1) * RC], b_k[:, h, cs], b_q[:, h, cs], start=True, stop=True)
                last.then_inc(S("b_scores"), 1)
            pe.wait_ge(S("b_masked"), nchunk)
            for c in range(nchunk):
                o_bank, s_bank = c % 2, 2 + c % 2
                if c:
                    pe.wait_ge(S("b_state"), c)
                if c >= 2:
                    pe.wait_ge(S("b_out"), c - 1)
                for h in range(GT):
                    hs_ = slice(h * RC, (h + 1) * RC)
                    last = nc.tensor.matmul(mp[:, o_bank, hs_], b_vn[:, c, h, :], b_sc[:, c, h, :], start=True, stop=(c == 0))
                    if c:
                        last = nc.tensor.matmul(mp[:, o_bank, hs_], b_s[:, h, :], b_qd[:, h, c * RC:(c + 1) * RC], start=False, stop=True)
                last.then_inc(S("b_inner"), 1)
                for h in range(GT):
                    last = nc.tensor.matmul(mp[:, s_bank, h * RC:(h + 1) * RC], b_kn[:, c, h, :], b_vn[:, c, h, :], start=True, stop=True)
                last.then_inc(S("b_kv"), 1)
            pe.wait_ge(S("b_out"), nchunk)
            pe.wait_ge(S("b_s_final"), 1)
            for h in range(GT):
                last = nc.tensor.matmul(mp[0:NS, 0, h * P:(h + 1) * P], b_v[:, h, NP:], ident[:, :], start=True, stop=True)
            last.then_inc(S("b_vst"), 1)
            pe.wait_ge(S("b_vsc"), 1)
            for b in range(NS):
                if b >= 2:
                    pe.wait_ge(S("b_st_new"), GT * (b - 1))
                nc.tensor.matmul(mp[:, 2 + b % 2, :], b_sel[0:NS, b, :], work[0:NS, 26864:27376],
                                 start=True, stop=True).then_inc(S("b_vb"), 1)
            pe.wait_ge(S("b_st_new"), NS * GT)
            for b in range(NS):
                for h in range(GT):
                    last = nc.tensor.matmul(mp[:, 1, h * NS + b:h * NS + b + 1], b_st[:, b, h, :], b_q[:, h, NP + b:NP + b + 1],
                                            start=True, stop=True)
            last.then_inc(S("b_os"), 1)
            norm_pe(pe, "b", ones, b_o, b_t, False)

        def b_dve(dve, lane):
            dve.wait_ge(S("b_loaded"), 16 * 7)
            for j in range(2 * GT):
                dve.wait_ge(S("b_swapped"), j + 1)
                nc.vector.tensor_tensor(halves(b_rot[:, j, :]), mp[:, (j % 2) * 2:(j % 2) * 2 + 2, 0:H2], halves(b_sin), ALU.mult).then_inc(S("b_sw"), 1)
                lane.done(nc.vector.tensor_tensor(b_in[:, j, :], b_in[:, j, :], b_cos, ALU.mult))
                dve.wait_ge(S("b_sw"), j + 1)
                ks = 1.0 if j < GT else float(RC) ** -0.5
                lane.done(nc.vector.tensor_tensor(b_in[:, j, :], b_in[:, j, :], b_rot[:, j, :], ALU.add))
                if j >= GT:
                    lane.done(nc.vector.tensor_scalar(b_in[:, j, :], b_in[:, j, :], ks, None, ALU.mult))
            for c in range(nchunk):
                cs = slice(c * RC, (c + 1) * RC)
                ins = nc.vector.tensor_tensor(b_qd[:, :, cs], b_q[:, :, cs], b_qdec, ALU.mult)
                if c < nchunk - 1:
                    lane.done(ins)
            lane.tell(ins, S("b_rotated"), 1)
            for c in range(nchunk):
                dve.wait_ge(S("b_tr"), 2 * c + 1)
                nc.vector.tensor_tensor(b_kn[:, c, :, :], bank((2 * c) % 4, GT, RC), b_kdec, ALU.mult).then_inc(S("b_nat"), 1)
                dve.wait_ge(S("b_tr"), 2 * c + 2)
                nc.vector.tensor_copy(b_vn[:, c, :, :], bank((2 * c + 1) % 4, GT, RC)).then_inc(S("b_nat"), 1)
            for c in range(nchunk):
                dve.wait_ge(S("b_scores"), c + 1)
                nc.vector.tensor_tensor(b_sc[:, c, :, :], bank(c, GT, RC), b_dmat, ALU.mult).then_inc(S("b_masked"), 1)
            for c in range(nchunk):
                dve.wait_ge(S("b_kv"), c + 1)
                for h in range(GT):
                    if c == 0:
                        ins = nc.vector.tensor_copy(b_s[:, h, :], mp[:, 2, h * P:(h + 1) * P])
                    else:
                        ins = nc.vector.scalar_tensor_tensor(out=b_s[:, h, :], in0=b_s[:, h, :], scalar=gam[h] ** RC,
                                                             in1=mp[:, 2 + c % 2, h * P:(h + 1) * P], op0=ALU.mult, op1=ALU.add)
                    if h < GT - 1:
                        lane.done(ins)
                lane.tell(ins, S("b_state"), c + 1)
                lane.tell(nc.vector.tensor_copy(b_o[:, :, c * RC:(c + 1) * RC], bank(c % 2, GT, RC)), S("b_out"), c + 1)
            lane.tell(nc.vector.tensor_copy(b_vs[0:1, 0, 0:1], b_o[0:1, 0, 0:1]), S("b_s_final"), 1)
            dve.wait_ge(S("b_vst"), 1)
            nc.vector.tensor_copy(work[0:NS, 26864:27376], mp[0:NS, 0, :]).then_inc(S("b_vsc"), 1)
            dve.wait_ge(S("b_st_dec"), GT)
            for b in range(NS):
                dve.wait_ge(S("b_vb"), b + 1)
                for h in range(GT):
                    nc.vector.scalar_tensor_tensor(out=b_st[:, b, h, :], in0=mp[:, 2 + b % 2, h * P:(h + 1) * P],
                                                   scalar=b_k[:, h, NP + b:NP + b + 1], in1=b_st[:, b, h, :],
                                                   op0=ALU.mult, op1=ALU.add).then_inc(S("b_st_new"), 1)
            dve.wait_ge(S("b_os"), 1)
            lane.tell(nc.vector.tensor_copy(b_o[:, :, NP:], mp[:, 1, 0:GT * NS].rearrange("p (a b) -> p a b", a=GT)), S("b_src"), 1)
            norm_dve(dve, lane, "b", b_o, b_t, RC, False)
            lane.tell(nc.vector.tensor_copy(b_vs[:, 0, 0:1], b_o[:, 0, 0:1]), S("b_normed"), 1)
            dve.wait_ge(S("b_sig"), 1)
            lane.done(nc.vector.tensor_tensor(b_o, b_o, b_t, ALU.mult))
            lane.tell(nc.vector.tensor_tensor(Y[:, 4:8, :], b_o, b_g, ALU.mult), S("b_done"), 1)

        cx_in = wk(0, NC_T, T)
        c_xs = wk(7280, NC_T, T)
        c_r, c_k, c_v = c_xs[:, 0:GT, :], c_xs[:, GT:2 * GT, :], c_xs[:, 2 * GT:3 * GT, :]
        c_a = wk(14560, GT, T)
        c_exc = wk(16640, GT, T)
        c_kk = wk(18720, GT, T)
        c_inc = wk(20800, GT, T)
        c_t = wk(22880, GT, T)
        c_o = wk(24960, GT, T)
        c_g2 = wk(27040, G)
        c_sg = wk(27552, T)
        c_wa = wk(28072, G)
        c_sh = wk(28584, NC_T, NS)
        cs_S, cs_p, cs_e = (wk(2048 * n, NS * GT, 64) for n in range(3))
        cs_v = wk(6144, NS * GT)
        x_kk, x_b, x_k, x_v, x_bc, x_kc = (wk(512 * n, GT, P) for n in range(6))
        n_b, n_k, n_v, n_kk = (wk(3072 + 512 * n, GT, P) for n in range(4))
        x_A, x_B = wk(5120, GT, P), wk(5632, GT, P)
        x_RB, x_RK, r_d, r_e = (wk(6144 + 256 * n, GT, CH) for n in range(4))
        c_S = wk(13520, GT, P)
        g_in, g_ex = wk(14032, GT, CH), wk(14288, GT, CH)
        x_Al, x_M, x_W, x_Y = (wk(22880 + 512 * n, GT, P) for n in range(4))
        x_MT, x_F, x_H = (wk(28072 + 512 * n, GT, P) for n in range(3))
        g_iv = wk(29608, GT, CH)
        n_tk, n_ty = n_kk, x_Y

        def over(t, n, w):
            return t.unsqueeze(1).broadcast_to([P, n, w])

        def c_act(act, lane):
            act.wait_ge(S("b_done"), 1)
            act.wait_ge(S("mix_stored"), 16 * (1 + GT + 2 + 2))
            act.dma_start(cx_in, pt[:, C0:C0 + NC_T, :]).then_inc(S("c_loaded"), 16)
            for t, n in ((c_sh, "st_shift"), (c_wa, "lora_wa"), (c_g2, "lora_g2")):
                act.dma_start(t, A[n]).then_inc(S("c_loaded"), 16)
            act.wait_ge(S("c_loaded"), 64)
            act.dma_start(O["shift"], cx_in[:, :, NP - 1:]).then_inc(S("mix_stored"), 16)
            act.wait_ge(S("c_shifted"), NC_T)
            nc.scalar.activation(c_xs[0:64, 12, :], c_xs[0:64, 12, :], ACT.Tanh).then_inc(S("c_act0"), 1)
            nc.scalar.activation(c_sg, c_xs[:, 13, :], ACT.Sigmoid).then_inc(S("c_act0"), 1)
            for n in range(GT):
                act.wait_ge(S("c_lora"), n + 1)
                nc.scalar.activation(halves(c_exc[:, n, :]), mp[:, 0:2, 0:H2], ACT.Sigmoid, bias=pr("w0", n)).then_inc(S("c_wa"), 1)
                nc.scalar.activation(halves(c_a[:, n, :]), mp[:, 2:4, 0:H2], ACT.Sigmoid, bias=pr("a0", n)).then_inc(S("c_wa"), 1)
            for n in range(GT):
                act.wait_ge(S("c_kk2"), n + 1)
                nc.scalar.activation(halves(c_t[:, n, :]), mp[:, (n % 2) * 2:(n % 2) * 2 + 2, 0:H2], ACT.Sqrt).then_inc(S("c_kkn"), 1)
            act.wait_ge(S("mix_stored"), 16 * (1 + GT + 2 + 2 + 1))
            act.wait_ge(S("c_vectors"), 1)
            act.dma_start(cs_S, A["st_wkv"]).then_inc(S("c_st_loaded"), 16)
            nc.scalar.activation(c_exc[:, :, NP:], c_exc[:, :, NP:], ACT.Exp).then_inc(S("c_sw"), 1)
            act.wait_ge(S("c_s_new"), 1)
            act.dma_start(O["wkv_s"], cs_S).then_inc(S("mix_stored"), 16)
            act.wait_ge(S("mix_stored"), 16 * (1 + GT + 2 + 2 + 1 + 1))
            lane.tell(nc.scalar.activation(g_in[:, 0, 0:1], epst[:, 0:1], ACT.Copy), S("c_area"), 1)
            with act.Fori(0, NP // CH) as i:
                ts = bass.ds(i * CH, CH)
                act.wait_ge(S("c_state"), i + 1)
                nc.scalar.activation(g_in, c_inc[:, :, ts], ACT.Exp).then_inc(S("c_g"), 1)
                nc.scalar.activation(g_iv, c_inc[:, :, ts], ACT.Exp, scale=-1.0).then_inc(S("c_g"), 1)
                nc.scalar.activation(g_ex, c_exc[:, :, ts], ACT.Exp).then_inc(S("c_g"), 1)
                act.wait_ge(S("c_tr"), i * 4 + 1)
                nc.scalar.activation(n_b, bank(0, GT, P), ACT.Copy).then_inc(S("c_na"), 1)
                act.wait_ge(S("c_tr"), i * 4 + 3)
                nc.scalar.activation(n_v, bank(2, GT, P), ACT.Copy).then_inc(S("c_na"), 1)
                act.wait_ge(S("c_Y"), i + 1)
                nc.scalar.activation(x_Y, bank(3, GT, P), ACT.Copy).then_inc(S("c_Yc"), 1)
                for l in range(1, LEVELS):
                    act.wait_ge(S("c_W"), i * (LEVELS - 1) + l)
                    nc.scalar.activation(x_W, bank(0, GT, P), ACT.Copy).then_inc(S("c_Wc"), 1)
                act.wait_ge(S("c_T"), i * 2 + 2)
                nc.scalar.activation(n_ty, bank(0, GT, P), ACT.Copy, scale=-1.0).then_inc(S("c_Tc"), 1)
                act.wait_ge(S("c_H"), i + 1)
                nc.scalar.activation(x_H, bank(3, GT, P), ACT.Copy).then_inc(S("c_Hc"), 1)
            act.wait_ge(S("c_state"), NP // CH + 1)
            act.dma_start(O["wkv_p"], c_S).then_inc(S("mix_stored"), 16)
            norm_act(act, "c", c_o, c_t, 64, 1, False)

        def c_pe(pe):
            pe.wait_ge(S("c_act0"), 2)
            for n in range(GT):
                if n:
                    pe.wait_ge(S("c_wa"), 2 * n)
                for b0, r0 in ((0, 0), (2, 64)):
                    for h, (c0, c1) in enumerate(two_halves):
                        last = nc.tensor.matmul(mp[:, b0 + h, 0:H2], c_wa[r0:r0 + 64, n * P:(n + 1) * P],
                                                c_xs[r0:r0 + 64, 12, c0:c1], start=True, stop=True)
                last.then_inc(S("c_lora"), 1)
            pe.wait_ge(S("c_wa"), 2 * GT)
            for n in range(GT):
                pe.wait_ge(S("c_kksq"), n + 1)
                if n >= 2:
                    pe.wait_ge(S("c_kkn"), n - 1)
                for h, (c0, c1) in enumerate(two_halves):
                    last = nc.tensor.matmul(mp[:, (n % 2) * 2 + h, 0:H2], blk[:, :], c_t[:, n, c0:c1], start=True, stop=True)
                last.then_inc(S("c_kk2"), 1)
            for n in range(5):
                pe.wait_ge(S("c_e"), n + 1)
                for q in range(4):
                    last = nc.tensor.matmul(mp[:, q, :], blk[:, :], work[:, 4096 + 512 * q:4096 + 512 * (q + 1)], start=True, stop=True)
                last.then_inc(S("c_eb"), 1)
            with pe.Fori(0, NP // CH) as i:
                def four(bk, pairs, w=P):
                    for p in range(GT):
                        for q, (a, b) in enumerate(pairs):
                            last = nc.tensor.matmul(mp[:, bk, p * w:(p + 1) * w], a(p), b(p), start=(q == 0), stop=(q == len(pairs) - 1))
                    return last

                def of(t):
                    return lambda p: t[:, p, :]

                pe.wait_ge(S("c_x"), i * 11 + 11)
                for n, x in enumerate((x_bc, x_kc, x_v, x_kk)):
                    for p in range(GT):
                        last = nc.tensor.transpose(mp[:, n, p * P:(p + 1) * P], x[:, p, :], ident[:, :])
                    last.then_inc(S("c_tr"), 1)
                pe.wait_ge(S("c_na"), i * 2 + 2)
                pe.wait_ge(S("c_nd"), i * 2 + 2)
                four(0, [(of(x_b), of(x_kk))]).then_inc(S("c_P"), 1)
                four(1, [(of(x_k), of(x_kk))]).then_inc(S("c_P"), 1)
                four(2, [(of(x_b), of(r_d))], CH).then_inc(S("c_P"), 1)
                four(3, [(of(x_k), of(r_d))], CH).then_inc(S("c_P"), 1)
                pe.wait_ge(S("c_A0"), i + 1)
                for p in range(GT):
                    last = nc.tensor.transpose(mp[:, 0, p * P:(p + 1) * P], x_Al[:, p, :], ident[:, :])
                last.then_inc(S("c_W0"), 1)
                pe.wait_ge(S("c_Pm"), i * 4 + 4)
                four(3, [(of(x_B), of(n_v))]).then_inc(S("c_Y"), 1)
                for l in range(1, LEVELS):
                    pe.wait_ge(S("c_Al"), i * (LEVELS - 1) + l)
                    pe.wait_ge(S("c_M"), i * (2 * LEVELS - 1) + 2 * l)
                    four(0, [(of(x_Al), of(x_M))]).then_inc(S("c_W"), 1)
                    pe.wait_ge(S("c_Wc"), i * (LEVELS - 1) + l)
                    if l < LEVELS - 1:
                        four(1, [(of(x_MT), of(x_W))]).then_inc(S("c_Z"), 1)
                    four(2, [(of(x_W), of(x_MT))]).then_inc(S("c_Z"), 1)
                pe.wait_ge(S("c_M"), i * (2 * LEVELS - 1) + (2 * LEVELS - 1))
                pe.wait_ge(S("c_Yc"), i + 1)
                four(0, [(of(x_MT), of(x_Y))]).then_inc(S("c_T"), 1)
                four(1, [(of(x_MT), of(n_kk))]).then_inc(S("c_T"), 1)
                pe.wait_ge(S("c_Tc"), i + 1)
                pe.wait_ge(S("c_Tk"), i + 1)
                four(2, [(of(n_tk), of(n_b))]).then_inc(S("c_F"), 1)
                four(3, [(of(n_k), of(n_v)), (of(n_b), of(n_ty))]).then_inc(S("c_H"), 1)
                four(0, [(of(n_tk), of(x_RB))], CH).then_inc(S("c_R"), 1)
                pe.wait_ge(S("c_Re"), i + 1)
                four(1, [(of(n_v), of(x_RK)), (of(n_ty), of(x_RB)), (of(c_S), of(r_e))], CH).then_inc(S("c_out"), 1)
                pe.wait_ge(S("c_Fc"), i * GT + GT)
                four(2, [(of(x_F), of(c_S))]).then_inc(S("c_new"), 1)
            norm_pe(pe, "c", blk, c_o, c_t, False)
            for n in range(GT):
                pe.wait_ge(S("c_rk"), n + 1)
                if n >= 2:
                    pe.wait_ge(S("c_bonus"), n - 1)
                for h, (c0, c1) in enumerate(two_halves):
                    last = nc.tensor.matmul(mp[:, (n % 2) * 2 + h, 0:H2], blk[:, :], c_a[:, n, c0:c1], start=True, stop=True)
                last.then_inc(S("c_rks"), 1)
            for n in range(GT):
                pe.wait_ge(S("c_bonus"), GT if n < 2 else GT + n - 1)
                for h, (c0, c1) in enumerate(two_halves):
                    last = nc.tensor.matmul(mp[:, (n % 2) * 2 + h, 0:H2], c_g2[:, n * P:(n + 1) * P], c_sg[:, c0:c1], start=True, stop=True)
                last.then_inc(S("c_gate"), 1)

        def c_dve(dve, lane):
            V = nc.vector
            dve.wait_ge(S("c_loaded"), 64)
            lane.done(V.tensor_tensor(c_xs[:, :, 1:NP], cx_in[:, :, 0:NP - 1], cx_in[:, :, 1:NP], ALU.subtract))
            lane.done(V.tensor_scalar(c_xs[:, :, 0], cx_in[:, :, 0], -1.0, None, ALU.mult))
            lane.done(V.tensor_tensor(c_xs[:, :, NP:], c_sh, cx_in[:, :, NP:], ALU.subtract))
            for j in range(NC_T):
                V.scalar_tensor_tensor(out=c_xs[:, j, :], in0=c_xs[:, j, :], scalar=pr("mu_c", j), in1=cx_in[:, j, :],
                                       op0=ALU.mult, op1=ALU.add).then_inc(S("c_shifted"), 1)
            dve.wait_ge(S("c_shifted"), NC_T)
            for j in range(GT):
                lane.done(V.tensor_scalar(c_kk[:, j, :], c_k[:, j, :], pr("k_k", j), None, ALU.mult))
                lane.tell(V.tensor_tensor(c_t[:, j, :], c_kk[:, j, :], c_kk[:, j, :], ALU.mult), S("c_kksq"), j + 1)
            for j in range(GT):
                dve.wait_ge(S("c_kkn"), j + 1)
                lane.done(V.tensor_scalar(c_t[:, j, :], c_t[:, j, :], 1e-12, None, ALU.max))
                lane.done(V.reciprocal(c_t[:, j, :], c_t[:, j, :]))
                lane.done(V.tensor_tensor(c_kk[:, j, :], c_kk[:, j, :], c_t[:, j, :], ALU.mult))
            dve.wait_ge(S("c_wa"), 2 * GT)
            lane.done(V.tensor_scalar(c_exc, c_exc, LD_SCALE, None, ALU.mult))
            for j in range(GT):
                lane.done(V.tensor_tensor_scan(c_inc[:, j, 0:NP], notfirst[:, :], c_exc[:, j, 0:NP], 0.0, ALU.mult, ALU.add))
                lane.done(V.tensor_tensor(c_exc[:, j, 0:NP], c_inc[:, j, 0:NP], c_exc[:, j, 0:NP], ALU.subtract))
                lane.done(V.tensor_scalar(c_t[:, j, :], c_a[:, j, :], -1.0, pr("k_a", j), ALU.add, ALU.mult))
                lane.done(V.scalar_tensor_tensor(out=c_k[:, j, :], in0=c_t[:, j, :], scalar=1.0, in1=c_k[:, j, :], op0=ALU.add, op1=ALU.mult))
                lane.done(V.tensor_tensor(c_a[:, j, :], c_a[:, j, :], c_kk[:, j, :], ALU.mult))
            lane.tell(V.memset(cs_v, 0.0), S("c_vectors"), 1)
            dve.wait_ge(S("c_st_loaded"), 16)
            dve.wait_ge(S("c_sw"), 1)
            e2 = eye2[:, :].unsqueeze(1).unsqueeze(1).broadcast_to([P, NS, GT, 64])
            four_d = "p (b g) j -> p b g j"

            def by_seq(t):
                return t[:, :, NP:].rearrange("p g b -> p b g").unsqueeze(3).broadcast_to([P, NS, GT, 64])

            sums = cs_v.rearrange("p (b g) -> p b g", b=NS)
            S4, p4, e4 = (t.rearrange(four_d, b=NS) for t in (cs_S, cs_p, cs_e))
            m4 = mp[:, :, :].rearrange("p q (b g j) -> p (q b) g j", b=2, g=GT)
            for n, vec in enumerate((c_kk, c_exc, c_a, c_k, c_r)):
                lane.tell(V.tensor_tensor(e4, e2, by_seq(vec), ALU.mult), S("c_e"), n + 1)
                dve.wait_ge(S("c_eb"), n + 1)
                if n == 0:
                    lane.done(V.tensor_tensor(p4, S4, m4, ALU.mult))
                    lane.done(V.tensor_reduce(cs_v, cs_p, AX, ALU.add))
                elif n == 1:
                    lane.done(V.tensor_tensor(S4, S4, m4, ALU.mult))
                elif n == 2:
                    lane.done(V.tensor_tensor(p4, m4, sums.unsqueeze(3).broadcast_to([P, NS, GT, 64]), ALU.mult))
                    lane.done(V.tensor_tensor(cs_S, cs_S, cs_p, ALU.subtract))
                elif n == 3:
                    lane.done(V.tensor_tensor(p4, m4, by_seq(c_v), ALU.mult))
                    lane.tell(V.tensor_tensor(cs_S, cs_S, cs_p, ALU.add), S("c_s_new"), 1)
                else:
                    lane.done(V.tensor_tensor(p4, S4, m4, ALU.mult))
                    lane.done(V.tensor_reduce(cs_v, cs_p, AX, ALU.add))
            lane.done(V.tensor_copy(c_o[:, :, NP:], sums.rearrange("p b g -> p g b")))
            dve.wait_ge(S("c_area"), 1)
            lane.done(V.memset(work[:, 0:3072], 0.0))
            lane.tell(V.memset(c_S, 0.0), S("c_state"), 1)
            eye4 = over(ident[:, :], GT, P)
            with dve.Fori(0, NP // CH) as i:
                ts = bass.ds(i * CH, CH)
                dve.wait_ge(S("c_g"), i * 3 + 3)
                for x, a, g in ((x_kk, c_kk, g_ex), (x_b, c_a, g_iv), (x_k, c_k, g_iv), (x_v, c_v, None)):
                    for h in range(2):
                        ps, cs_ = slice(64 * h, 64 * h + 64), slice(CH * h, CH * h + CH)
                        if g is None:
                            ins = V.tensor_copy(x[ps, :, cs_], a[ps, :, ts])
                        else:
                            ins = V.tensor_tensor(x[ps, :, cs_], a[ps, :, ts], g[ps, :, :], ALU.mult)
                        ins.then_inc(S("c_x"), 1)
                V.tensor_tensor(r_d, c_r[:, :, ts], g_in, ALU.mult).then_inc(S("c_x"), 1)
                dve.wait_ge(S("c_x"), i * 11 + 9)
                end = g_in[:, :, CH - 1:CH].broadcast_to([P, GT, P])
                V.tensor_tensor(x_bc, x_b, end, ALU.mult).then_inc(S("c_x"), 1)
                V.tensor_tensor(x_kc, x_k, end, ALU.mult).then_inc(S("c_x"), 1)
                dve.wait_ge(S("c_tr"), i * 4 + 2)
                V.tensor_copy(n_k, bank(1, GT, P)).then_inc(S("c_nd"), 1)
                dve.wait_ge(S("c_tr"), i * 4 + 4)
                V.tensor_copy(n_kk, bank(3, GT, P)).then_inc(S("c_nd"), 1)
                def masked(n, x, m, w):
                    dve.wait_ge(S("c_P"), i * 4 + (n + 1))
                    V.tensor_tensor(x, bank(n, GT, w), over(m[:, :], GT, w), ALU.mult).then_inc(S("c_Pm"), 1)

                masked(0, x_A, m_lt, P)
                dve.wait_ge(S("c_Pm"), i * 4 + 1)
                V.tensor_tensor(x_Al, x_A, over(m_lv[:, 0:P], GT, P), ALU.mult).then_inc(S("c_A0"), 1)
                dve.wait_ge(S("c_A0"), i + 1)
                V.tensor_tensor(x_MT, eye4, x_Al, ALU.subtract).then_inc(S("c_M"), 1)
                masked(1, x_B, m_lt, P)
                masked(2, x_RB, m_le, CH)
                masked(3, x_RK, m_le, CH)
                dve.wait_ge(S("c_W0"), i + 1)
                V.tensor_tensor(x_M, eye4, bank(0, GT, P), ALU.subtract).then_inc(S("c_M"), 1)
                per = 2 * LEVELS - 1
                dve.wait_ge(S("c_M"), i * per + 1)
                for l in range(1, LEVELS):
                    V.tensor_tensor(x_Al, x_A, over(m_lv[:, l * P:(l + 1) * P], GT, P), ALU.mult).then_inc(S("c_Al"), 1)
                    dve.wait_ge(S("c_M"), i * per + 2 * l)
                    if l < LEVELS - 1:
                        dve.wait_ge(S("c_Z"), i * (per - 2) + (2 * l))
                        V.tensor_tensor(x_M, x_M, bank(1, GT, P), ALU.subtract).then_inc(S("c_M"), 1)
                    else:
                        dve.wait_ge(S("c_Z"), i * (per - 2) + (2 * l - 1))
                    V.tensor_tensor(x_MT, x_MT, bank(2, GT, P), ALU.subtract).then_inc(S("c_M"), 1)
                dve.wait_ge(S("c_T"), i * 2 + 2)
                V.tensor_copy(n_tk, bank(1, GT, P)).then_inc(S("c_Tk"), 1)
                dve.wait_ge(S("c_F"), i + 1)
                for p in range(GT):
                    V.scalar_tensor_tensor(out=x_F[:, p, :], in0=ident[:, :], scalar=g_in[:, p, CH - 1:CH], in1=mp[:, 2, p * P:(p + 1) * P],
                                           op0=ALU.mult, op1=ALU.subtract).then_inc(S("c_Fc"), 1)
                dve.wait_ge(S("c_R"), i + 1)
                V.tensor_tensor(r_e, r_d, bank(0, GT, CH), ALU.subtract).then_inc(S("c_Re"), 1)
                dve.wait_ge(S("c_out"), i + 1)
                V.tensor_copy(c_o[:, :, ts], bank(1, GT, CH)).then_inc(S("c_oc"), 1)
                dve.wait_ge(S("c_new"), i + 1)
                dve.wait_ge(S("c_Hc"), i + 1)
                V.tensor_tensor(c_S, bank(2, GT, P), x_H, ALU.add).then_inc(S("c_state"), 1)
            dve.wait_ge(S("c_state"), NP // CH + 1)
            dve.wait_ge(S("c_oc"), NP // CH)
            lane.tell(V.tensor_copy(work[:, 29608:29609], c_o[:, 0, 0:1]), S("c_src"), 1)
            norm_dve(dve, lane, "c", c_o, c_t, 64, False)
            for j in range(GT):
                lane.done(V.tensor_scalar(c_o[:, j, :], c_o[:, j, :], pr("lnx_g", j), pr("lnx_b", j), ALU.mult, ALU.add))
                lane.tell(V.scalar_tensor_tensor(out=c_a[:, j, :], in0=c_r[:, j, :], scalar=pr("r_k", j), in1=c_k[:, j, :],
                                                 op0=ALU.mult, op1=ALU.mult), S("c_rk"), j + 1)
            for j in range(GT):
                dve.wait_ge(S("c_rks"), j + 1)
                lane.done(V.tensor_tensor(halves(c_a[:, j, :]), mp[:, (j % 2) * 2:(j % 2) * 2 + 2, 0:H2], halves(c_v[:, j, :]), ALU.mult))
                lane.tell(V.tensor_tensor(c_o[:, j, :], c_o[:, j, :], c_a[:, j, :], ALU.add), S("c_bonus"), j + 1)
            for j in range(GT):
                dve.wait_ge(S("c_gate"), j + 1)
                lane.tell(V.tensor_tensor(halves(Y[:, 8 + j, :]), mp[:, (j % 2) * 2:(j % 2) * 2 + 2, 0:H2], halves(c_o[:, j, :]), ALU.mult),
                          S("c_bonus"), GT + j + 1)

        def act_mix(act, lane):
            act.wait_ge(S("stored0"), 16 * (2 * KT + IN_T) // 2 + 16)
            act.wait_ge(S("stored1"), 16 * (2 * KT + IN_T) // 2 + 16)
            d_act(act, lane)
            a_act(act, lane)
            b_act(act, lane)
            c_act(act, lane)
            act.wait_ge(S("c_bonus"), 2 * GT)
            act.wait_ge(S("mix_stored"), 16 * (1 + GT + 2 + 2 + 1 + 1 + 1))

        def pe_mix(pe):
            d_pe(pe)
            pe.wait_ge(S("d_done"), 1)
            b_pe(pe)
            pe.wait_ge(S("b_done"), 1)
            c_pe(pe)

        def dve_mix(dve, lane):
            d_dve(dve, lane)
            a_dve(dve, lane)
            b_dve(dve, lane)
            c_dve(dve, lane)

        k_t = wk(0, KT, NM)
        v_t = wk(8192, KT, NM)
        v_n = wk(4096, 2, KT * P)
        s_kv = (wk(8192, KT * NM), wk(12288, KT * NM))
        p_r = wk(OFF_SQ, NP // P, NM)
        p_t = wk(OFF_SQ + 1024, 2, NP)
        p_m = wk(OFF_SQ + 2048, 3, NP // P)
        s_s = wk(OFF_SQ + 2064, 2, NS * 4)
        s_r = wk(OFF_SQ + 2128, NM)
        s_pt = wk(OFF_SQ + 2384, 2, NS * 4)
        s_m = wk(OFF_SQ + 2448, 4)
        HT = KT // 4

        def act_attn(act, lane):
            act.wait_ge(unit_done, U_O)
            act.wait_ge(evac, 2 * KT + IN_T + 2 * KT + 2)
            act.dma_start(v_t, O["mem_v"]).then_inc(S("kv_loaded"), 16)
            act.dma_start(k_t, O["mem_k"]).then_inc(S("kv_loaded"), 16)
            for h in range(4):
                act.wait_ge(S("t_bias"), h + 1)
                for t in range(NP // P):
                    nc.scalar.activation(p_r[:, t, :], mp[:, t // 2, (t % 2) * NM:(t % 2 + 1) * NM], ACT.Exp, scale=XA_SCALE,
                                         bias=p_m[:, 1, t:t + 1], accum_out=p_m[:, 2, t:t + 1]).then_inc(S("t_exp"), 1)
            act.wait_ge(S("v_nat"), 8)
            for n in range(2 * NS):
                if n >= 2:
                    act.wait_ge(S("cache_used"), n - 1)
                act.dma_start(s_kv[n % 2], A["cache_k" if n < NS else "cache_v"][n % NS]).then_inc(S(f"cache_loaded{n % 2}"), 16)
                if n == NS + 1:
                    act.wait_ge(S("s_bias"), 1)
                    nc.scalar.activation(s_r[0:32, :], mp[0:32, 2, 0:NM], ACT.Exp, scale=XA_SCALE, bias=s_m[0:32, 1:2],
                                         accum_out=s_m[0:32, 2:3]).then_inc(S("s_exp"), 1)

        def pe_attn(pe):
            pe.wait_ge(S("kv_loaded"), 32)
            for n in range(8):
                if n >= 4:
                    pe.wait_ge(S("v_nat"), n - 3)
                for j in range(4):
                    k = (n % 4) * 4 + j
                    last = nc.tensor.transpose(mp[:, n % 4, j * P:(j + 1) * P], v_t[:, k, (n // 4) * P:(n // 4 + 1) * P], ident[:, :])
                last.then_inc(S("v_tr"), 1)
            pe.wait_ge(S("v_nat"), 8)
            pe.wait_ge(evac, 2 * KT + IN_T + 2 * KT + 2)
            for h in range(4):
                if h:
                    pe.wait_ge(S("t_out"), h * HT)
                for t in range(NP // P):
                    for d in range(HT):
                        last = nc.tensor.matmul(mp[:, t // 2, (t % 2) * NM:(t % 2 + 1) * NM], Y[:, h * HT + d, t * P:(t + 1) * P],
                                                k_t[:, h * HT + d, :], start=(d == 0), stop=(d == HT - 1))
                last.then_inc(S("t_scores"), 1)
                pe.wait_ge(S("t_norm"), h + 1)
                for m in range(2):
                    for t in range(NP // P):
                        last = nc.tensor.transpose(mp[:, 2 + m, t * P:(t + 1) * P], p_r[:, t, m * P:(m + 1) * P], ident[:, :])
                last.then_inc(S("t_tr"), 1)
                pe.wait_ge(S("t_pt"), h + 1)
                for d in range(HT):
                    if d >= 2:
                        pe.wait_ge(S("t_out"), h * HT + d - 1)
                    for m in range(2):
                        k = h * HT + d
                        last = nc.tensor.matmul(mp[:, d % 2, :], v_n[:, m, k * P:(k + 1) * P], p_t[:, m, :], start=(m == 0), stop=(m == 1))
                    last.then_inc(S("t_o"), 1)
            pe.wait_ge(S("t_out"), 4 * HT)
            for b in range(NS):
                pe.wait_ge(S(f"cache_loaded{b % 2}"), 16 * (b // 2 + 1))
                kc = s_kv[b % 2].rearrange("p (k m) -> p k m", k=KT)
                for h in range(4):
                    for m in range(2):
                        for d in range(HT):
                            k = h * HT + d
                            col = m * 32 + b * 4 + h
                            last = nc.tensor.matmul(mp[:, 0, col:col + 1], kc[:, k, m * P:(m + 1) * P], Y[:, k, NP + b:NP + b + 1],
                                                    start=(d == 0), stop=(d == HT - 1))
                last.then_inc(S("cache_used"), 1)
            pe.wait_ge(S("s_sc"), 1)
            for m in range(2):
                last = nc.tensor.matmul(mp[0:32, 2, m * P:(m + 1) * P], s_s[:, m, :], ident[:, :], start=True, stop=True)
            last.then_inc(S("s_tr"), 1)
            pe.wait_ge(S("s_norm"), 1)
            for m in range(2):
                last = nc.tensor.matmul(mp[:, 3, m * 32:(m + 1) * 32], s_r[0:32, m * P:(m + 1) * P], ident[0:32, 0:32], start=True, stop=True)
            last.then_inc(S("s_trb"), 1)
            pe.wait_ge(S("s_ptc"), 1)
            for b in range(NS):
                pe.wait_ge(S(f"cache_loaded{b % 2}"), 16 * (b // 2 + 1 + NS // 2))
                vc = s_kv[b % 2].rearrange("p (m c) -> p m c", m=2)
                for k in range(KT):
                    for m in range(2):
                        h = k // HT
                        last = nc.tensor.matmul(mp[:, 1, k * NS + b:k * NS + b + 1], vc[:, m, k * P:(k + 1) * P],
                                                s_pt[:, m, b * 4 + h:b * 4 + h + 1], start=(m == 0), stop=(m == 1))
                last.then_inc(S("cache_used"), 1)

        def dve_attn(dve, lane):
            V = nc.vector
            for n in range(8):
                dve.wait_ge(S("v_tr"), n + 1)
                V.tensor_copy(v_n[:, n // 4, (n % 4) * 512:(n % 4 + 1) * 512], mp[:, n % 4, :]).then_inc(S("v_nat"), 1)
            for h in range(4):
                dve.wait_ge(S("t_scores"), h + 1)
                lane.done(V.tensor_reduce(p_m[:, 0, :], mp[:, 0:2, :].rearrange("p a (b m) -> p (a b) m", b=2), AX, ALU.max))
                lane.tell(V.tensor_scalar(p_m[:, 1, :], p_m[:, 0, :], -XA_SCALE, None, ALU.mult), S("t_bias"), h + 1)
                dve.wait_ge(S("t_exp"), (h + 1) * (NP // P))
                lane.done(V.reciprocal(p_m[:, 2, :], p_m[:, 2, :]))
                lane.tell(V.tensor_tensor(p_r, p_r, p_m[:, 2, :].unsqueeze(2).broadcast_to([P, NP // P, NM]), ALU.mult), S("t_norm"), h + 1)
                dve.wait_ge(S("t_tr"), h + 1)
                V.tensor_copy(p_t, mp[:, 2:4, :]).then_inc(S("t_pt"), 1)
                for d in range(HT):
                    dve.wait_ge(S("t_o"), h * HT + d + 1)
                    V.tensor_copy(Y[:, h * HT + d, 0:NP], mp[:, d % 2, :]).then_inc(S("t_out"), 1)
            dve.wait_ge(S("cache_used"), NS)
            lane.tell(V.tensor_copy(s_s, mp[:, 0, 0:64].rearrange("p (m c) -> p m c", m=2)), S("s_sc"), 1)
            dve.wait_ge(S("s_tr"), 1)
            lane.done(V.tensor_reduce(s_m[0:32, 0:1], mp[0:32, 2, 0:NM], AX, ALU.max))
            lane.tell(V.tensor_scalar(s_m[0:32, 1:2], s_m[0:32, 0:1], -XA_SCALE, None, ALU.mult), S("s_bias"), 1)
            dve.wait_ge(S("s_exp"), 1)
            lane.done(V.reciprocal(s_m[0:32, 2:3], s_m[0:32, 2:3]))
            lane.tell(V.tensor_scalar(s_r[0:32, :], s_r[0:32, :], s_m[0:32, 2:3], None, ALU.mult), S("s_norm"), 1)
            dve.wait_ge(S("s_trb"), 1)
            lane.tell(V.tensor_copy(s_pt, mp[:, 3, 0:64].rearrange("p (m c) -> p m c", m=2)), S("s_ptc"), 1)
            dve.wait_ge(S("cache_used"), 2 * NS)
            lane.done(V.tensor_copy(Y[:, :, NP:], mp[:, 1, 0:KT * NS].rearrange("p (k b) -> p k b", k=KT)))
            lane.tell(V.memset(s_m[0:32, 3:4], 0.0), S("attn_done"), 1)

        block = ctx.enter_context(nc.Block())

        @block.sync
        def _(sp):
            def load(w, n, u, s):
                sp.wait_ge(hi_ready, u - (RING - 1))
                sp.wait_ge(lo_ready, u - (RING - 1))
                sp.dma_start(raw[:, s, :], w[bass.ds(n, 1)].rearrange("a p n -> (a p) n")).then_inc(raw_landed[s], 16)

            for s in range(RING):
                sp.dma_start(raw[:, s, :], A["w_k"][s]).then_inc(raw_landed[s], 16)
            for name, u0, first in (("w_k", U_KV, 1), ("w_v", U_KV + 2 * KT, 0), ("w_in", U_IN, 0), ("w_out", U_OUT, 0),
                                    ("w_q", U_Q, 0), ("w_o", U_O, 0)):
                with sp.Fori(first, A[name].shape[0] // RING) as i:
                    for s in range(RING):
                        load(A[name], i * RING + s, i * RING + (u0 + s), s)
            with sp.Fori(0, FB) as f:
                u = f * (2 * FT + KT)
                with sp.Fori(0, 2 * FT // RING) as i:
                    for s in range(RING):
                        load(A["w_up"], f * (2 * FT) + i * RING + s, u + i * RING + (U_MLP + s), s)
                with sp.Fori(0, KT // RING) as i:
                    for s in range(RING):
                        load(A["w_down"], f * KT + i * RING + s, u + i * RING + (U_MLP + 2 * FT + s), s)

        @block.gpsimd
        def _(pool):
            with pool.Fori(0, UNITS // RING) as i:
                for s in range(RING):
                    pool.wait_ge(hi_ready, i * RING + (s + 1))
                    nc.gpsimd.tensor_tensor(lo[:, s, :], raw[:, s, :], hi[:, s, :].bitcast(F32), ALU.subtract).then_inc(lo_ready, 1)

        @block.tensor
        def _(pe):
            def product(t, par, units, u, moving, cols, split=None):
                pe.wait_ge(evac, t + 1)
                last_unit = len(units) - 1
                for q, (s, k0) in enumerate(units):
                    pe.wait_ge(lo_ready, u + (q + 1))
                    if split and q == 1:
                        pe.wait_ge(S("xl"), split)
                    for kt in range(UK):
                        wh = hi[:, s, kt * P:(kt + 1) * P]
                        wl = lo[:, s, kt * P:(kt + 1) * P]
                        mh, ml = moving(k0 + kt)
                        for w, m, a, b in ((wh, mh, kt == 0 and q == 0, False), (wh, ml, False, False),
                                           (wl, mh, False, kt == UK - 1 and q == last_unit)):
                            for h, (c0, c1) in enumerate(cols):
                                last = nc.tensor.matmul(gp[:, par, h, 0:c1 - c0], w, m[:, c0:c1], start=a, stop=b)
                    last.then_inc(unit_done, 1)

            def x_moving(k):
                return xh[:, k, :], xl[:, k, :]

            def u_moving(k):
                return uh[:, k, :], ul[:, k, :]

            two = ((0, H2), (H2, T))

            def gemm(name, tiles, t0, u0, cols=two):
                split = at("xl", name) + KT
                pe.wait_ge(S("xl"), split - KT + UK)
                with pe.Fori(0, tiles // 2) as i:
                    for s in range(2):
                        product(i * 2 + (t0 + s), s, ((2 * s, 0), (2 * s + 1, UK)), i * 4 + (u0 + 2 * s), x_moving, cols, split)

            def sum_squares(name, n, cols):
                pe.wait_ge(S("acc"), n + at("acc", name))
                for h, (c0, c1) in enumerate(cols):
                    last = nc.tensor.matmul(mp[:, h, 0:c1 - c0], ones[:, :], acc[:, c0:c1], start=True, stop=True)
                return last

            mem = ((0, NM),)
            pe.wait_ge(S("const_loaded"), 16 * 11)
            sum_squares("mem", KT + 1, mem).then_inc(S("ss"), 1)
            gemm("mem", 2 * KT, 0, U_KV, mem)
            sum_squares("x", KT + 1, two).then_inc(S("ss"), 1)
            gemm("x", IN_T, 2 * KT, U_IN)
            pe_mix(pe)
            t0 = 2 * KT + IN_T
            gemm("y", KT, t0, U_OUT)
            sum_squares("o", KT + 1, two).then_inc(S("ss"), 1)
            gemm("o", KT, t0 + KT, U_Q)
            pe_attn(pe)
            gemm("a", KT, t0 + 2 * KT, U_O)
            sum_squares("m", KT + 1, two).then_inc(S("ss"), 1)
            pe.wait_ge(S("xl"), KT + at("xl", "m"))
            t0 += 3 * KT
            with pe.Fori(0, FB) as f:
                for j in range(FT // 2):
                    for s in range(2):
                        product(f * (FT + KT) + (t0 + 2 * j + s), s, ((2 * s, 0), (2 * s + 1, UK)),
                                f * (2 * FT + KT) + (U_MLP + 4 * j + 2 * s), x_moving, two)
                with pe.Fori(0, KT // 4) as j:
                    for s in range(4):
                        if s == 0:
                            pe.wait_ge(S("ul"), f * FT + (FT + 2))
                        product(f * (FT + KT) + j * 4 + (t0 + FT + s), s % 2, ((s, 0),),
                                f * (2 * FT + KT) + j * 4 + (U_MLP + 2 * FT + s), u_moving, two)
            sum_squares("f", KT + 1, two).then_inc(S("ss"), 1)

        @block.scalar
        def _(act):
            lane = Lane(act, S("act_lane"))

            def split(i, ubase, s):
                act.wait_ge(raw_landed[s], i * 16 + 16 * (ubase // RING + 1))
                if not (isinstance(i, int) and ubase + RING * i < RING):
                    act.wait_ge(unit_done, i * RING + (ubase + s - (RING - 1)))
                nc.scalar.activation(hi[:, s, :], raw[:, s, :], ACT.Copy).then_inc(hi_ready, 1)

            def squares_and_hi(name, src, n, g, do_sq=True):
                for k in range(KT):
                    if k >= 2 and do_sq:
                        act.wait_ge(S("acc"), k + at("acc", name))
                    if do_sq:
                        nc.scalar.activation(sq[:, k % 2, 0:n], src(k), ACT.Square).then_inc(S("sq"), 1)
                    sc = pr(g, k) if g else 1.0
                    nc.scalar.activation(xh[:, k, 0:n], src(k), ACT.Copy, scale=sc).then_inc(S("xh"), 1)

            def root(k, n, mean, cols):
                act.wait_ge(S("ss"), k)
                for h, (c0, c1) in enumerate(cols):
                    ins = nc.scalar.activation(rstd[:, c0:c1], mp[:, h, 0:c1 - c0], ACT.Sqrt, scale=1.0 / mean, bias=epst[:, 0:1])
                    if h < len(cols) - 1:
                        lane.done(ins)
                lane.tell(ins, S("root"), k)

            two = ((0, H2), (H2, T))
            for n, t in (("ident", ident), ("ones", ones), ("swap", swap), ("blk", blk), ("eye2", eye2), ("m_lt", m_lt),
                         ("m_le", m_le), ("m_lv", m_lv), ("notfirst", notfirst), ("eps", epst)):
                c, w = CST[n]
                act.dma_start(t[:, :], A["consts"][:, c:c + w]).then_inc(S("const_loaded"), 16)
            act.dma_start(prm[:, :], A["params"]).then_inc(S("const_loaded"), 16)
            act.dma_start(X[:, :, 0:NM], A["mem_t"]).then_inc(S("mem_loaded"), 16)
            act.wait_ge(S("const_loaded"), 16 * 11)
            act.wait_ge(S("mem_loaded"), 16)
            squares_and_hi("mem", lambda k: X[:, k, 0:NM], NM, "g_mem")
            for s in range(RING):
                split(0, 0, s)
            root(1, NM, DM, ((0, NM),))

            def store_loop(tiles, t0, u0, dst, n, sem):
                with act.Fori(0, tiles // 2) as i:
                    for s in range(2):
                        split(i, u0 + RING, 2 * s)
                        split(i, u0 + RING, 2 * s + 1)
                        act.wait_ge(evac, i * 2 + (t0 + s + 3))
                        act.dma_start(dst(i * 2 + s), stg[:, s, 0:n]).then_inc(S(f"{sem}{s}"), 16)

            store_loop(KT, 0, U_KV, lambda n: O["mem_k"][:, bass.ds(n, 1), :].rearrange("p a t -> p (a t)"), NM, "stored")
            with act.Fori(0, KT // 2) as i:
                for s in range(2):
                    split(i, U_KV + 2 * KT + RING, 2 * s)
                    split(i, U_KV + 2 * KT + RING, 2 * s + 1)
                    act.wait_ge(evac, i * 2 + (KT + s + 3))
                    act.dma_start(O["mem_v"][:, bass.ds(i * 2 + s, 1), :].rearrange("p a t -> p (a t)"),
                                  stg[:, s, 0:NM]).then_inc(S(f"stored{s}"), 16)
            act.wait_ge(unit_done, U_IN)
            act.wait_ge(S("xl"), KT + at("xl", "mem"))
            act.dma_start(X, A["x_t"]).then_inc(S("x_loaded"), 16)
            act.wait_ge(S("x_loaded"), 16)
            squares_and_hi("x", lambda k: X[:, k, :], T, "g_mix")
            root(2, T, DM, two)
            store_loop(IN_T, 2 * KT, U_IN, lambda n: pt[:, bass.ds(n, 1), :].rearrange("p a t -> p (a t)"), T, "stored")
            act_mix(act, lane)
            act.dma_start(X, A["x_t"]).then_inc(S("x_loaded"), 16)
            squares_and_hi("y", lambda k: Y[:, k, :], T, None, do_sq=False)

            def residual_loop(tiles, t0, u0, name):
                with act.Fori(0, tiles // 2) as i:
                    for s in range(2):
                        split(i, u0 + RING, 2 * s)
                        split(i, u0 + RING, 2 * s + 1)
                        act.wait_ge(evac, i * 2 + (t0 + s + 3))
                        act.wait_ge(S("acc"), (i * 2 + (s + 1)) + at("acc", name))
                        nc.scalar.activation(sq[:, s, :], tile(X, i * 2 + s), ACT.Square).then_inc(S("sq"), 1)

            t0 = 2 * KT + IN_T
            residual_loop(KT, t0, U_OUT, "o")

            def rescale(name):
                act.wait_ge(S("acc"), (KT + 1) + at("acc", name[0]))
                act.wait_ge(unit_done, name[2])
                for k in range(KT):
                    nc.scalar.activation(xh[:, k, :], X[:, k, :], ACT.Copy, scale=pr(name[1], k)).then_inc(S("xh"), 1)
                root(name[3], T, DM, two)

            rescale(("o", "g_xa", U_Q, 3))
            with act.Fori(0, KT // 2) as i:
                for s in range(RING):
                    split(i, U_Q + RING, s)
            act_attn(act, lane)
            act.wait_ge(S("attn_done"), 1)
            squares_and_hi("a", lambda k: Y[:, k, :], T, None, do_sq=False)
            residual_loop(KT, t0 + 2 * KT, U_O, "m")
            rescale(("m", "g_mlp", U_MLP, 4))
            t0 += 3 * KT
            hid = wk(OFF_MISC, 2, T)
            usq = wk(OFF_SQ, 2, T)
            per = 2 * FT + KT

            def mlp_block(f, peel):
                for j in range(FT // 2):
                    for s in range(2):
                        for q in range(2):
                            split(f * (per // RING) + (j + 1), U_MLP, 2 * s + q)
                        act.wait_ge(evac, f * (FT + KT) + (t0 + 2 * j + s + 3))
                        act.wait_ge(S("ul"), f * FT + (2 * j + s + 1))
                        nc.scalar.activation(usq[:, s, :], hid[:, s, :], ACT.Square).then_inc(S("usq"), 1)
                        act.wait_ge(S("usq"), f * FT + (2 * j + s + 1))
                        nc.scalar.activation(uh[:, 2 * j + s, :], usq[:, s, :], ACT.Copy).then_inc(S("uh"), 1)
                for j in range(KT // 4):
                    if peel and j == KT // 4 - 1:
                        break
                    for s in range(RING):
                        split(f * (per // RING) + (FT // 2 + j + 1), U_MLP, s)

            with act.Fori(0, FB - 1) as f:
                mlp_block(f, False)
            mlp_block(FB - 1, True)
            for k in range(KT):
                if k == 0:
                    act.wait_ge(evac, t0 + FB * (FT + KT) + 2)
                if k >= 2:
                    act.wait_ge(S("acc"), k + at("acc", "f"))
                nc.scalar.activation(sq[:, k % 2, :], X[:, k, :], ACT.Square).then_inc(S("sq"), 1)
            root(5, T, DM, two)
            act.wait_ge(S("y_final"), KT)
            act.dma_start(O["y_t"], X).then_inc(S("y_stored"), 16)
            act.wait_ge(S("y_stored"), 16)
            act.wait_ge(S("stored0"), 16 * (2 * KT + IN_T) // 2 + 16)
            act.wait_ge(S("stored1"), 16 * (2 * KT + IN_T) // 2 + 16)

        @block.vector
        def _(dve):
            lane = Lane(dve, S("dve_lane"))
            nc.vector.memset(stg[:, 0, 0:1], 0.0).then_inc(evac, 2)
            nc.vector.memset(stg[:, 0, 1:2], 0.0).then_inc(S("stored0"), 16)
            nc.vector.memset(stg[:, 1, 0:1], 0.0).then_inc(S("stored1"), 16)
            dve.wait_ge(evac, 2)
            dve.wait_ge(S("stored0"), 16)
            dve.wait_ge(S("stored1"), 16)
            dve.wait_ge(S("const_loaded"), 16 * 11)

            def accumulate(name, k, n):
                dve.wait_ge(S("sq"), (k + 1) + at("sq", name))
                dve.wait_ge(S("acc"), (k + 1) + at("acc", name))
                nc.vector.tensor_tensor(acc[:, 0:n], acc[:, 0:n], sq[:, k % 2, 0:n], ALU.add).then_inc(S("acc"), 1)

            def lows(name, src, n, g, do_sq=True):
                if do_sq:
                    nc.vector.memset(acc[:, 0:n], 0.0).then_inc(S("acc"), 1)
                for k in range(KT):
                    dve.wait_ge(S("xh"), (k + 1) + at("xh", name))
                    if g:
                        nc.vector.scalar_tensor_tensor(out=xl[:, k, 0:n], in0=src(k), scalar=pr(g, k), in1=xh[:, k, 0:n].bitcast(F32),
                                                       op0=ALU.mult, op1=ALU.subtract).then_inc(S("xl"), 1)
                    else:
                        nc.vector.tensor_tensor(xl[:, k, 0:n], src(k), xh[:, k, 0:n].bitcast(F32), ALU.subtract).then_inc(S("xl"), 1)
                    if do_sq:
                        accumulate(name, k, n)

            def invert(k, n):
                dve.wait_ge(S("root"), k)
                lane.done(nc.vector.reciprocal(rstd[:, 0:n], rstd[:, 0:n]))

            def stage_loop(tiles, t0, u0, n):
                with dve.Fori(0, tiles // 2) as i:
                    for s in range(2):
                        dve.wait_ge(unit_done, i * 4 + (u0 + 2 * s + 2))
                        dve.wait_ge(S(f"stored{s}"), i * 16 + (16 * t0 // 2 + 16))
                        if n == NM:
                            nc.vector.tensor_tensor(stg[:, s, 0:n], gp[:, s, 0, 0:n], rstd[:, 0:n], ALU.mult).then_inc(evac, 1)
                        else:
                            nc.vector.tensor_tensor(halves(stg[:, s, :]), gphalf(s), halves(rstd[:, :]), ALU.mult).then_inc(evac, 1)

            dve.wait_ge(S("mem_loaded"), 16)
            lows("mem", lambda k: X[:, k, 0:NM], NM, "g_mem")
            invert(1, NM)
            stage_loop(2 * KT, 0, U_KV, NM)
            dve.wait_ge(S("x_loaded"), 16)
            lows("x", lambda k: X[:, k, :], T, "g_mix")
            invert(2, T)
            stage_loop(IN_T, 2 * KT, U_IN, T)
            dve_mix(dve, lane)
            lows("y", lambda k: Y[:, k, :], T, None, do_sq=False)
            dve.wait_ge(S("x_loaded"), 32)

            def residual_loop(tiles, t0, u0, name):
                nc.vector.memset(acc[:, :], 0.0).then_inc(S("acc"), 1)
                with dve.Fori(0, tiles // 2) as i:
                    for s in range(2):
                        dve.wait_ge(unit_done, i * 4 + (u0 + 2 * s + 2))
                        x = halves(tile(X, i * 2 + s))
                        nc.vector.tensor_tensor(x, gphalf(s), x, ALU.add).then_inc(evac, 1)
                        dve.wait_ge(S("sq"), (i * 2 + (s + 1)) + at("sq", name))
                        dve.wait_ge(S("acc"), (i * 2 + (s + 1)) + at("acc", name))
                        nc.vector.tensor_tensor(acc[:, :], acc[:, :], sq[:, s, :], ALU.add).then_inc(S("acc"), 1)

            def lows_of_x(name, g):
                for k in range(KT):
                    dve.wait_ge(S("xh"), (k + 1) + at("xh", name))
                    nc.vector.scalar_tensor_tensor(out=xl[:, k, :], in0=X[:, k, :], scalar=pr(g, k), in1=xh[:, k, :].bitcast(F32),
                                                   op0=ALU.mult, op1=ALU.subtract).then_inc(S("xl"), 1)

            t0 = 2 * KT + IN_T
            residual_loop(KT, t0, U_OUT, "o")
            lows_of_x("o", "g_xa")
            invert(3, T)
            with dve.Fori(0, KT // 2) as i:
                for s in range(2):
                    dve.wait_ge(unit_done, i * 4 + (U_Q + 2 * s + 2))
                    nc.vector.tensor_tensor(halves(tile(Y, i * 2 + s)), gphalf(s), halves(rstd[:, :]), ALU.mult).then_inc(evac, 1)
            dve_attn(dve, lane)
            lows("a", lambda k: Y[:, k, :], T, None, do_sq=False)
            residual_loop(KT, t0 + 2 * KT, U_O, "m")
            lows_of_x("m", "g_mlp")
            invert(4, T)
            t0 += 3 * KT
            hid = wk(OFF_MISC, 2, T)
            usq = wk(OFF_SQ, 2, T)
            per = 2 * FT + KT
            nc.vector.memset(stg[:, 0, 0:1], 0.0).then_inc(S("ul"), 2)
            dve.wait_ge(S("ul"), 2)
            with dve.Fori(0, FB) as f:
                for j in range(FT // 2):
                    for s in range(2):
                        n = 2 * j + s
                        dve.wait_ge(unit_done, f * per + (U_MLP + 4 * j + 2 * s + 2))
                        nc.vector.scalar_tensor_tensor(out=halves(hid[:, s, :]), in0=gphalf(s), scalar=0.0, in1=halves(rstd[:, :]),
                                                       op0=ALU.max, op1=ALU.mult).then_inc(evac, 1)
                        dve.wait_ge(S("uh"), f * FT + (n + 1))
                        nc.vector.tensor_tensor(ul[:, n, :], usq[:, s, :], uh[:, n, :].bitcast(F32), ALU.subtract).then_inc(S("ul"), 1)
                with dve.Fori(0, KT // 4) as j:
                    for s in range(4):
                        dve.wait_ge(unit_done, f * per + j * 4 + (U_MLP + 2 * FT + s + 1))
                        x = halves(tile(X, j * 4 + s))
                        nc.vector.tensor_tensor(x, gphalf(s % 2), x, ALU.add).then_inc(evac, 1)
            dve.wait_ge(evac, t0 + FB * (FT + KT) + 2)
            nc.vector.memset(acc[:, :], 0.0).then_inc(S("acc"), 1)
            for k in range(KT):
                accumulate("f", k, T)
            invert(5, T)
            for k in range(KT):
                nc.vector.scalar_tensor_tensor(out=X[:, k, :], in0=X[:, k, :], scalar=pr("g_final", k), in1=rstd[:, :],
                                               op0=ALU.mult, op1=ALU.mult).then_inc(S("y_final"), 1)


_COLS = {"A": (0, 1536), "B": (1536, 3584), "C": (3584, 5376), "D": (5376, 6400)}


def _tiles(a):
    a = np.asarray(a)
    a = a.reshape(a.shape[:-1] + (a.shape[-1] // P, P))
    return np.moveaxis(np.moveaxis(a, -1, 0), -1, 1)


def _untile(a):
    a = np.moveaxis(np.moveaxis(a, 1, -1), 0, -1)
    return a.reshape(a.shape[:-2] + (-1,))


def _units(w, k_tiles):
    k, n = w.shape
    u = w.reshape(k_tiles // UK, UK, P, n // P, P).transpose(3, 0, 2, 1, 4)
    return u.reshape(-1, P, UK * P)


def _layout(i):
    c = np.ascontiguousarray
    w_in = np.concatenate([i["w_in"][0][:, _COLS[g][0]:_COLS[g][1]] for g in "CBDA"], 1)
    prm = {n: i[n][0] for n in ("g_mix", "g_xa", "g_mem", "g_mlp", "mu_c", "w0", "a0", "k_k", "k_a", "r_k", "lnx_g",
                                "lnx_b", "conv_a_w", "conv_d_b", "ln_d_g", "ln_d_b")}
    prm = {n: _tiles(a).reshape(P, -1) if a.ndim == 1 else a.reshape(-1, GT, P).transpose(2, 0, 1).reshape(P, -1)
           for n, a in prm.items()}
    prm["g_final"] = _tiles(i["g_final"])
    prm["conv_d_w"] = i["conv_d_w"][0].reshape(TAPS, GT, P).transpose(2, 1, 0).reshape(P, -1)
    x = np.concatenate([i["x_prompt"][0], i["x_sample"][:, 0]], 0)
    return {
        "w_k": c(_units(i["wk_x"][0], KT)), "w_v": c(_units(i["wv_x"][0], KT)), "w_in": c(_units(w_in, KT)),
        "w_out": c(_units(i["w_out"][0], KT)), "w_q": c(_units(i["wq_x"][0], KT)), "w_o": c(_units(i["wo_x"][0], KT)),
        "w_up": c(_units(i["w_up"][0], KT)),
        "w_down": np.concatenate([_units(i["w_down"][0][f * FT * P:(f + 1) * FT * P], FT) for f in range(FB)], 0),
        "params": c(np.concatenate([prm[n] for n in PRM], 1)),
        "consts": np.concatenate(list(constants().values()), 1),
        "x_t": c(_tiles(x)),
        "mem_t": c(_tiles(i["mem_prompt"][0])),
        "lora_wa": np.concatenate([i["w2"][0], i["a2"][0]], 0),
        "lora_g2": c(i["g2"][0]),
        "st_a": c(i["state_conv_a"][0].reshape(NS, 2, GT, P).transpose(3, 2, 1, 0)),
        "st_d": c(i["state_conv_d"][0].reshape(NS, TAPS - 1, GT, P).transpose(3, 2, 0, 1)),
        "st_shift": c(_tiles(i["state_shift"][0])),
        "st_ret": c(i["state_ret"][0].transpose(2, 0, 1, 3)),
        "st_wkv": c(i["state_wkv"][0].reshape(NS, GT, 2, 64, 64).transpose(2, 3, 0, 1, 4).reshape(P, NS * GT, 64)),
        "cache_k": c(i["cache_mem_k"][0].reshape(NS, NM, KT, P).transpose(0, 3, 2, 1).reshape(NS, P, -1)),
        "cache_v": c(i["cache_mem_v"][0].reshape(NS, 2, P, KT * P).transpose(0, 2, 1, 3).reshape(NS, P, -1)),
    }


_OUT = {"y_t": (P, KT, T), "mem_k": (P, KT, NM), "mem_v": (P, KT, NM), "conv_a_p": (P, GT, 2), "conv_a_s": (P, GT, 2, NS),
        "conv_d_p": (P, GT, TAPS - 1), "conv_d_s": (P, GT, NS, TAPS - 1), "shift": (P, NC_T, 1 + NS),
        "ret_p": (P, GT, P), "ret_s": (P, NS, GT, P), "wkv_p": (P, GT, P), "wkv_s": (P, NS * GT, 64)}


def kernel(**inputs):
    import concourse.bacc as bacc
    from concourse.bass_utils import run_bass_kernel_spmd

    arrays = _layout({n: np.asarray(a) for n, a in inputs.items()})
    nc = bacc.Bacc("TRN2", target_bir_lowering=False, num_devices=1)
    dev_in = {n: nc.dram_tensor(f"in_{n}", a.shape, F32, kind="ExternalInput").ap() for n, a in arrays.items()}
    dev_out = {n: nc.dram_tensor(f"out_{n}", s, F32, kind="ExternalOutput").ap() for n, s in _OUT.items()}
    program(nc, dev_in, dev_out)
    r = run_bass_kernel_spmd(nc, [{f"in_{n}": a for n, a in arrays.items()}], core_ids=[0]).results[0]
    o = {n: r[f"out_{n}"] for n in _OUT}

    shift = _untile(o["shift"])
    y = _untile(o["y_t"])
    wkv_p = np.stack([o["wkv_p"][64 * h:64 * h + 64, :, 64 * h:64 * h + 64] for h in range(2)], 0)
    return (
        y[None, :NP], y[NP:, None],
        o["conv_a_p"].transpose(2, 1, 0).reshape(1, 1, 2, G),
        o["conv_a_s"].transpose(3, 2, 1, 0).reshape(1, NS, 2, G),
        o["ret_p"].transpose(1, 0, 2)[None, None], o["ret_s"].transpose(1, 2, 0, 3)[None],
        shift[None, :1], shift[None, 1:],
        wkv_p.transpose(2, 0, 3, 1).reshape(1, 1, 8, 64, 64),
        o["wkv_s"].reshape(2, 64, NS, GT, 64).transpose(2, 3, 0, 1, 4).reshape(1, NS, 8, 64, 64),
        o["conv_d_p"].transpose(2, 1, 0).reshape(1, 1, TAPS - 1, G),
        o["conv_d_s"].transpose(2, 3, 1, 0).reshape(1, NS, TAPS - 1, G),
        o["mem_k"].transpose(2, 1, 0).reshape(1, 1, NM, 4, 512), o["mem_v"].transpose(2, 1, 0).reshape(1, 1, NM, 4, 512),
    )
```
